# Optimizing a Trainium2 kernel written in Bass

```python
import jax, jax.numpy as jnp
from jax import lax
import numpy as np

D_MODEL = 2048
BATCH = 1
SEQ = 512
DEPTH = 1
DEC_BATCH = 1
DEC_SEQ = 64
PAST_LEN = 1024

CHUNK = 64
N_HEADS = D_MODEL // 256
HEAD_DIM = 128
D_ATTN = N_HEADS * HEAD_DIM
D_CONV = D_MODEL // 2
CONV_WIDTH = 31
Q_BLOCK = 128
EPS = 1e-6
D_IN = 4 * D_ATTN + N_HEADS + 3 * D_CONV + 2 * D_MODEL

kernel_name = "fox_conformer_gated_hybrid_stream_step"

def _split_points():
    sizes = (D_ATTN, D_ATTN, D_ATTN, N_HEADS, D_ATTN, 2 * D_CONV, D_CONV, D_MODEL, D_MODEL)
    return np.cumsum(np.array(sizes))[:-1].tolist()

def _rmsnorm(x, g):
    xf = x.astype(jnp.float32)
    y = xf * lax.rsqrt(jnp.mean(xf * xf, axis=-1, keepdims=True) + EPS) * g.astype(jnp.float32)
    return y.astype(x.dtype)

def _layernorm(x, g, b):
    xf = x.astype(jnp.float32)
    mu = jnp.mean(xf, axis=-1, keepdims=True)
    var = jnp.mean(jnp.square(xf - mu), axis=-1, keepdims=True)
    y = (xf - mu) * lax.rsqrt(var + EPS) * g.astype(jnp.float32) + b.astype(jnp.float32)
    return y.astype(x.dtype)

def _fox_prompt(q, k, v, logf):
    B, S, H, Dh = q.shape
    scale = Dh ** -0.5
    F = jnp.cumsum(logf, axis=1).transpose(0, 2, 1)
    nb = S // Q_BLOCK
    qb = q.reshape(B, nb, Q_BLOCK, H, Dh).transpose(1, 0, 2, 3, 4)
    Fb = F.reshape(B, H, nb, Q_BLOCK).transpose(2, 0, 1, 3)
    pos_k = jnp.arange(S)

    def one_block(args):
        i, qi, Fi = args
        s = jnp.einsum('bqhd,bkhd->bhqk', qi, k, preferred_element_type=jnp.float32) * scale
        bias = Fi[..., :, None] - F[..., None, :]
        pos_q = i * Q_BLOCK + jnp.arange(Q_BLOCK)
        mask = pos_k[None, :] <= pos_q[:, None]
        s = jnp.where(mask, s + bias, -jnp.inf)
        p = jax.nn.softmax(s, axis=-1)
        return jnp.einsum('bhqk,bkhd->bqhd', p.astype(v.dtype), v)

    out = lax.map(one_block, (jnp.arange(nb), qb, Fb))
    return out.transpose(1, 0, 2, 3, 4).reshape(B, S, H * Dh)

def _fox_sample(q, k_new, v_new, logf_new, k_cache, v_cache, logf_cache):
    B, T, H, Dh = q.shape
    P = k_cache.shape[1]
    scale = Dh ** -0.5
    k_all = jnp.concatenate([k_cache.astype(k_new.dtype), k_new], axis=1)
    v_all = jnp.concatenate([v_cache.astype(v_new.dtype), v_new], axis=1)
    logf_all = jnp.concatenate([logf_cache.astype(jnp.float32), logf_new], axis=1)
    F = jnp.cumsum(logf_all, axis=1).transpose(0, 2, 1)
    Fq = F[:, :, P:]
    s = jnp.einsum('bqhd,bkhd->bhqk', q, k_all, preferred_element_type=jnp.float32) * scale
    bias = Fq[..., :, None] - F[..., None, :]
    pos_k = jnp.arange(P + T)
    pos_q = P + jnp.arange(T)
    mask = pos_k[None, :] <= pos_q[:, None]
    s = jnp.where(mask, s + bias, -jnp.inf)
    p = jax.nn.softmax(s, axis=-1)
    out = jnp.einsum('bhqk,bkhd->bqhd', p.astype(v_all.dtype), v_all)
    return out.reshape(B, T, H * Dh)

def _depthwise_causal(u, buf, w, b):
    ext = jnp.concatenate([buf.astype(u.dtype), u], axis=1)
    y = lax.conv_general_dilated(ext, w[:, None, :].astype(u.dtype), window_strides=(1,), padding='VALID',
                                 dimension_numbers=('NWC', 'WIO', 'NWC'), feature_group_count=u.shape[-1])
    return y + b, ext[:, -(CONV_WIDTH - 1):]

def _layer(x, c, k_cache, v_cache, logf_cache, conv_buf,
           w_ada, b_ada, norm_g, w_in, b_f, q_g, k_g,
           conv_w, conv_b, ln_g, ln_b, w_oa, w_ob, w_out):
    B, T, _ = x.shape
    mod = jnp.einsum('bd,de->be', jax.nn.silu(c), w_ada) + b_ada
    shift, scale, gate = jnp.split(mod, 3, axis=-1)
    h = _rmsnorm(x, norm_g) * (1 + scale[:, None]) + shift[:, None]
    z = jnp.einsum('btd,de->bte', h, w_in)
    q, k, v, f_logit, g_a, glu_in, g_b, m_a, m_b = jnp.split(z, _split_points(), axis=-1)
    q = _rmsnorm(q.reshape(B, T, N_HEADS, HEAD_DIM), q_g)
    k = _rmsnorm(k.reshape(B, T, N_HEADS, HEAD_DIM), k_g)
    v = v.reshape(B, T, N_HEADS, HEAD_DIM)
    logf = jax.nn.log_sigmoid((f_logit + b_f).astype(jnp.float32))

    if k_cache is None:
        attn = _fox_prompt(q, k, v, logf)
        buf0 = jnp.zeros((B, CONV_WIDTH - 1, D_CONV), x.dtype)
    else:
        attn = _fox_sample(q, k, v, logf, k_cache, v_cache, logf_cache)
        buf0 = conv_buf
    y_a = attn * jax.nn.silu(g_a)

    ga_lin, ga_gate = jnp.split(glu_in, 2, axis=-1)
    u = ga_lin * jax.nn.sigmoid(ga_gate)
    cv, new_buf = _depthwise_causal(u, buf0, conv_w, conv_b)
    cv = jax.nn.silu(_layernorm(cv, ln_g, ln_b))
    y_b = cv * jax.nn.silu(g_b)

    p_a = jnp.einsum('btc,cd->btd', y_a, w_oa)
    p_b = jnp.einsum('btc,cd->btd', y_b, w_ob)
    merged = jax.nn.sigmoid(m_a) * p_a + jax.nn.sigmoid(m_b) * p_b
    out = jnp.einsum('btd,de->bte', merged, w_out)
    x = x + gate[:, None] * out
    return x, k, v, logf, new_buf

def setup_inputs(seed: int = 0) -> dict:
    key = jax.random.key(seed)
    ks = jax.random.split(key, 24)
    n = jax.random.normal
    D = D_MODEL
    return {
        "x_prompt": n(ks[0], (BATCH, SEQ, D), jnp.float32),
        "x_sample": n(ks[1], (DEC_BATCH, DEC_SEQ, D), jnp.float32),
        "c_prompt": n(ks[2], (BATCH, D), jnp.float32),
        "c_sample": n(ks[3], (DEC_BATCH, D), jnp.float32),
        "cache_k": n(ks[4], (DEPTH, DEC_BATCH, PAST_LEN, N_HEADS, HEAD_DIM), jnp.float32),
        "cache_v": n(ks[5], (DEPTH, DEC_BATCH, PAST_LEN, N_HEADS, HEAD_DIM), jnp.float32),
        "cache_logf": jax.nn.log_sigmoid(3.0 + 0.5 * n(ks[6], (DEPTH, DEC_BATCH, PAST_LEN, N_HEADS), jnp.float32)),
        "state_conv": 0.5 * n(ks[7], (DEPTH, DEC_BATCH, CONV_WIDTH - 1, D_CONV), jnp.float32),
        "w_ada": 0.3 * D ** -0.5 * n(ks[8], (DEPTH, D, 3 * D), jnp.float32),
        "b_ada": 0.02 * n(ks[9], (DEPTH, 3 * D), jnp.float32),
        "norm_g": 1.0 + 0.05 * n(ks[10], (DEPTH, D), jnp.float32),
        "w_in": D ** -0.5 * n(ks[11], (DEPTH, D, D_IN), jnp.float32),
        "b_f": 3.0 + 0.5 * n(ks[12], (DEPTH, N_HEADS), jnp.float32),
        "q_norm_g": 1.0 + 0.05 * n(ks[13], (DEPTH, HEAD_DIM), jnp.float32),
        "k_norm_g": 1.0 + 0.05 * n(ks[14], (DEPTH, HEAD_DIM), jnp.float32),
        "conv_w": CONV_WIDTH ** -0.5 * n(ks[15], (DEPTH, CONV_WIDTH, D_CONV), jnp.float32),
        "conv_b": 0.02 * n(ks[16], (DEPTH, D_CONV), jnp.float32),
        "conv_ln_g": 1.0 + 0.05 * n(ks[17], (DEPTH, D_CONV), jnp.float32),
        "conv_ln_b": 0.02 * n(ks[18], (DEPTH, D_CONV), jnp.float32),
        "w_oa": D_ATTN ** -0.5 * n(ks[19], (DEPTH, D_ATTN, D), jnp.float32),
        "w_ob": D_CONV ** -0.5 * n(ks[20], (DEPTH, D_CONV, D), jnp.float32),
        "w_out": D ** -0.5 * n(ks[21], (DEPTH, D, D), jnp.float32),
    }

def reference(x_prompt, x_sample, c_prompt, c_sample, cache_k, cache_v, cache_logf, state_conv,
              w_ada, b_ada, norm_g, w_in, b_f, q_norm_g, k_norm_g, conv_w, conv_b,
              conv_ln_g, conv_ln_b, w_oa, w_ob, w_out):
    xp, xs = x_prompt, x_sample
    kp, vp, fp, cp = [], [], [], []
    ksm, vsm, fsm, csm = [], [], [], []
    for l in range(DEPTH):
        wl = (w_ada[l], b_ada[l], norm_g[l], w_in[l], b_f[l], q_norm_g[l], k_norm_g[l],
              conv_w[l], conv_b[l], conv_ln_g[l], conv_ln_b[l], w_oa[l], w_ob[l], w_out[l])
        xp, k1, v1, f1, b1 = _layer(xp, c_prompt, None, None, None, None, *wl)
        xs, k2, v2, f2, b2 = _layer(xs, c_sample, cache_k[l], cache_v[l], cache_logf[l], state_conv[l], *wl)
        kp.append(k1); vp.append(v1); fp.append(f1); cp.append(b1)
        ksm.append(k2); vsm.append(v2); fsm.append(f2); csm.append(b2)
    return (xp, xs,
            jnp.stack(kp), jnp.stack(vp), jnp.stack(fp), jnp.stack(cp),
            jnp.stack(ksm), jnp.stack(vsm), jnp.stack(fsm), jnp.stack(csm))


_drawn_inputs = setup_inputs


def setup_inputs(seed=0):
    import zlib

    import numpy as np

    out = dict(_drawn_inputs(seed))
    spreads = {}
    factors = {'cache_k': 8.0,
     'cache_v': 8.0,
     'cache_logf': 8.0,
     'state_conv': 3.671,
     'q_norm_g': 8.0,
     'conv_b': 8.0,
     'conv_ln_g': 27.187,
     'conv_ln_b': 64.0}
    for name, (base, spread) in spreads.items():
        noise = np.random.default_rng([zlib.crc32(name.encode()), seed]).standard_normal(out[name].shape)
        drawn = base * np.exp(spread * noise) if base else spread * noise
        out[name] = __import__('jax').numpy.asarray(drawn.astype(out[name].dtype))
    for name, factor in factors.items():
        out[name] = (out[name] * factor).astype(out[name].dtype)
    return out
```

```python
from contextlib import ExitStack

import concourse.bass as bass
from concourse import mybir

F32 = mybir.dt.float32
F32R = mybir.dt.float32r
ACT = mybir.ActivationFunctionType
ALU = mybir.AluOpType
AX = mybir.AxisListType

P = 128
D = 2048
KT = D // P
NP = 512
NS = 64
T = NP + NS
HC = T // 2
H = 8
PAST = 1024
CT = PAST // P
QB = NP // P
W = 31
PADW = W - 1
EXT = 2 * PADW + T
ACCW = EXT - PADW
S_ST = PADW + NP
S_U = S_ST + PADW
EPS = 1e-6
SCALE = float(P) ** -0.5
MASKED = -1e30
G_PAST = NP
G_NEW = NP + PAST
GW = NP + PAST + NS

UK = 8
UW = UK * P
RING = 4
LEAD = 3
AHEAD = 7
ADA_UNITS = 2 * 2 * KT
ADA_USES = ADA_UNITS // RING
A_TILES = 8
A_STEPS = 2 * A_TILES
B_TURNS = (2 * KT - H) // 2
N_A = H * A_STEPS
N_B = 4 * B_TURNS
N_C = 2 * KT
N_D = 2 * KT
N_UNITS = N_A + N_B + N_C + N_D
B0, C0, D0 = N_A, N_A + N_B, N_A + N_B + N_C
X, Y, Z, V = 4, 5, 6, 7


def build(nc, a, o):
    ctx = ExitStack()
    with ctx:
        top = [((nc.sbuf_base + 63) // 64) * 64]

        def room(nbytes):
            at = top[0]
            top[0] += (nbytes + 31) // 32 * 32
            return at

        def place(name, shape, at, dt=F32):
            return nc.alloc_sbuf_tensor_at(name, shape, dt, offset=at)

        def sb(name, shape, dt=F32):
            n = 4
            for s in shape[1:]:
                n *= s
            return place(name, shape, room(n), dt)

        TB = T * 4
        w_raw = sb("w_raw", [P, RING, UW])
        w_hi = sb("w_hi", [P, RING, UW], F32R)
        w_lo = sb("w_lo", [P, RING, UW], F32R)
        ones = sb("ones", [P, P])
        ident = sb("ident", [P, P])
        upto = sb("upto", [P, P])
        after = sb("after", [P, P])
        causal = sb("causal", [P, P])
        eps_c = sb("eps_c", [P, 1])
        c_in = sb("c_in", [P, KT, 2])
        c_silu = sb("c_silu", [P, KT, 2])
        b_ada = sb("b_ada", [P, 3 * KT])
        norm_g = sb("norm_g", [P, KT])
        mod = sb("mod", [P, 2 * KT, 2])
        gate = sb("gate", [P, KT, 2])
        qk_g = sb("qk_g", [P, 2])
        ln_gb = sb("ln_gb", [P, H, 2])
        ln_cur = sb("ln_cur", [P, 2])
        w_f = sb("w_f", [P, KT, H])
        w_f_hi = sb("w_f_hi", [P, KT, H], F32R)
        w_f_lo = sb("w_f_lo", [P, KT, H], F32R)
        b_f = sb("b_f", [P, 5, H])
        z_f = sb("z_f", [P, 5, H])
        e_f = sb("e_f", [P, 5, H])
        logf = sb("logf", [P, 5, H])
        logf_past = sb("logf_past", [P, CT, H])
        conv_w = sb("conv_w", [P, W + 1])
        stat_max = sb("stat_max", [P, 5])
        stat_neg = sb("stat_neg", [P, 5])
        stat_sum = sb("stat_sum", [P, 5])
        stat_inv = sb("stat_inv", [P, 5])
        ch_sum = sb("ch_sum", [P, T])

        h_hi_at = room(KT * TB)
        h_lo_at = room(KT * TB)
        x_at = room((2 * H + 1) * TB)
        s_at = top[0]
        h_hi = place("h_hi", [P, KT, T], h_hi_at, F32R)
        h_lo = place("h_lo", [P, KT, T], h_lo_at, F32R)
        x_t = place("x_t", [P, KT, T], x_at)
        y_a = place("y_a", [P, H, T], x_at)
        cv = place("cv", [P, H + 1, T], x_at + H * TB)
        yb_hi = place("yb_hi", [P, H, T], h_hi_at, F32R)
        yb_lo = place("yb_lo", [P, H, T], h_hi_at + H * TB, F32R)
        mg_hi = place("mg_hi", [P, KT, T], h_lo_at, F32R)
        mg_lo = place("mg_lo", [P, KT, T], x_at, F32R)

        sq_x = place("sq_x", [P, 4, T], s_at)
        rstd_x = place("rstd_x", [P, T], s_at + 4 * TB)
        g_rows = place("g_rows", [H, GW], s_at + 5 * TB)
        g_b = sb("g_b", [P, GW])
        qn = sb("qn", [P, T])
        kn = sb("kn", [P, T])
        vf = sb("vf", [P, T])
        sq = sb("sq", [P, T])
        rs = sb("rs", [P, T])
        v_tok = sb("v_tok", [P, QB + 1, P])
        past = sb("past", [P, PAST])
        s_p = sb("s_p", [P, 2, NP])
        s_s = sb("s_s", [P, PAST + NS])
        p_t = sb("p_t", [P, QB, P])
        ps_t = sb("ps_t", [P, CT, NS])
        pn_t = sb("pn_t", [NS, NS])
        s_gb = sb("s_gb", [P, T])
        sig = sb("sig", [P, T])
        ext = sb("ext", [P, EXT])
        acc = sb("acc", [P, ACCW])
        s_m_at = top[0]
        s_m = sb("s_m", [P, T])
        end_a = top[0]
        top[0] = s_at
        ya_hi = sb("ya_hi", [P, H, T], F32R)
        ya_lo = sb("ya_lo", [P, H, T], F32R)
        b_at = top[0]
        assert b_at + 4 * TB <= s_m_at
        mu = place("mu", [P, T], b_at)
        rstd = place("rstd", [P, T], b_at + TB)
        sq_b = place("sq_b", [P, T], b_at + 2 * TB)
        sq_sum = place("sq_sum", [P, T], b_at + 3 * TB)
        gb_at = end_a
        gb_in = place("gb_in", [P, 2, T], gb_at)
        m_in = place("m_in", [P, 2, 2, T], b_at)
        merge_at = b_at + 4 * TB
        merge = place("merge", [P, T], merge_at)
        merge_b = place("merge_b", [P, T], x_at + 2 * H * TB)
        w_gate = place("w_gate", [P, 2, UW], merge_at + TB)
        x_in = place("x_in", [P, 2, T], b_at)
        y_out = place("y_out", [P, 2, T], b_at + 2 * TB)

        ps = ctx.enter_context(nc.psum_tensor("ps", [P, 8, 512], F32))
        g_dram = nc.dram_tensor("g_scratch", [H, GW], F32, kind="Internal").ap()
        gb_dram = nc.dram_tensor("silu_gb_scratch", [H, P, T], F32, kind="Internal").ap()
        m_dram = nc.dram_tensor("sigmoid_m_scratch", [2 * KT, P, T], F32, kind="Internal").ap()

        def sem(name):
            return ctx.enter_context(nc.semaphore(name))

        const_in = sem("const_in")
        x_landed = sem("x_landed")
        masks_ready = sem("masks_ready")
        pool_step = sem("pool_step")
        zeroed = sem("zeroed")
        w_landed = [sem(f"w_landed{r}") for r in range(RING)]
        ada_used = sem("ada_used")
        hi_ready, lo_ready, w_used = sem("hi_ready"), sem("lo_ready"), sem("w_used")
        tile_evac = sem("tile_evac")
        silu_c = sem("silu_c")
        sqx_ready, sqx_used = sem("sqx_ready"), sem("sqx_used")
        rstdx_ready = sem("rstdx_ready")
        xn_ready = sem("xn_ready")
        mod_ready = sem("mod_ready")
        h_ready, h_hi_ready, h_lo_ready = sem("h_ready"), sem("h_hi_ready"), sem("h_lo_ready")
        wf_hi_ready, wf_lo_ready = sem("wf_hi_ready"), sem("wf_lo_ready")
        f_done, f_act, logf_ready, logf_stored = sem("f_done"), sem("f_act"), sem("logf_ready"), sem("logf_stored")
        g_done, g_rows_ready, g_stored, g_landed = sem("g_done"), sem("g_rows_ready"), sem("g_stored"), sem("g_landed")
        sq_ready, ss_done, std_ready = sem("sq_ready"), sem("ss_done"), sem("std_ready")
        qkn_ready, k_stored, v_stored = sem("qkn_ready"), sem("k_stored"), sem("v_stored")
        vt_done, vtok_ready = sem("vt_done"), sem("vtok_ready")
        past_landed = sem("past_landed")
        sc_done, sc_evac, prep_done, exp_done, p_ready = (sem(n) for n in ("sc_done", "sc_evac", "prep_done", "exp_done", "p_ready"))
        tr_done, pt_ready, pv_done, pv_evac = (sem(n) for n in ("tr_done", "pt_ready", "pv_done", "pv_evac"))
        u_ready, conv_done, cw_landed, c_stored = (sem(n) for n in ("u_ready", "conv_done", "cw_landed", "c_stored"))
        gb_stored, m_stored = sem("gb_stored"), sem("m_stored")
        summed = sem("summed")
        mean_done, mu_ready = sem("mean_done"), sem("mu_ready")
        centred, sqb_ready, sq_summed = sem("centred"), sem("sqb_ready"), sem("sq_summed")
        var_done, rstd_ready = sem("var_done"), sem("rstd_ready")
        lncur_ready, scaled, ln_silu = sem("lncur_ready"), sem("scaled"), sem("ln_silu")
        gb_landed = [sem(f"gb_landed{r}") for r in range(2)]
        yb_ready, ya_hi_ready, ya_lo_ready = sem("yb_ready"), sem("ya_hi_ready"), sem("ya_lo_ready")
        yb_hi_ready, yb_lo_ready = sem("yb_hi_ready"), sem("yb_lo_ready")
        m_landed = [sem(f"m_landed{r}") for r in range(2)]
        gate_landed = [sem(f"gate_landed{r}") for r in range(2)]
        gate_used, gate_ready = sem("gate_used"), sem("gate_ready")
        merged, mg_hi_ready, mg_lo_ready = sem("merged"), sem("mg_hi_ready"), sem("mg_lo_ready")
        c_evac = sem("c_evac")
        xin_landed = [sem(f"xin_landed{r}") for r in range(2)]
        y_ready, y_stored = sem("y_ready"), [sem(f"y_stored{r}") for r in range(2)]
        inv_done = sem("inv_done")
        chain = sem("dve_step")

        def banks(b):
            return ps[:, b:b + 2, 0:HC]

        def halves(ap):
            return ap.rearrange("p (c n) -> p c n", c=2)

        def uses(n):
            return 16 * (ADA_USES + n + 1)

        block = ctx.enter_context(nc.Block())

        @block.sync
        def _(sp):
            for dst, src in ((c_in, a["c"]), (b_ada, a["b_ada"]), (norm_g, a["norm_g"]), (qk_g, a["qk_g"]),
                             (ln_gb, a["ln_gb"]), (w_f, a["w_f"]), (b_f, a["b_f"]), (logf_past, a["logf_past"])):
                sp.dma_start(dst[:], src).then_inc(const_in, 16)
            for g in range(4):
                sp.dma_start(x_t[:, 4 * g:4 * g + 4], a["x"][:, 4 * g:4 * g + 4]).then_inc(x_landed, 16)
            for r in range(RING):
                sp.dma_start(w_raw[:, r], a["w_ada"][r]).then_inc(w_landed[r], 16)
            with sp.Fori(0, ADA_USES - 1) as i:
                for r in range(RING):
                    sp.wait_ge(ada_used, 4 * i + r + 1)
                    sp.dma_start(w_raw[:, r], a["w_ada"][4 * i + r + 4]).then_inc(w_landed[r], 16)

            def load_unit(n, slot):
                sp.dma_start(w_raw[:, slot], a["w"][n]).then_inc(w_landed[slot], 16)

            for n in range(RING):
                sp.wait_ge(ada_used, ADA_UNITS - RING + n + 1)
                load_unit(n, n)
            for n in range(RING, AHEAD):
                sp.wait_ge(lo_ready, n - RING + 1)
                load_unit(n, n % RING)
            sp.wait_ge(logf_ready, 1)
            sp.dma_start(o["logf_p"], logf[:, 0:QB]).then_inc(logf_stored, 16)
            sp.dma_start(o["logf_s"], logf[NS:P, QB]).then_inc(logf_stored, 16)
            sp.wait_ge(g_rows_ready, 4)
            sp.dma_start(g_dram, g_rows[:]).then_inc(g_stored, 16)
            sp.wait_ge(g_stored, 16)

            with sp.Fori(0, H) as i:
                for u in range(A_STEPS):
                    sp.wait_ge(lo_ready, A_STEPS * i + u + AHEAD - RING + 1)
                    load_unit(A_STEPS * i + u + AHEAD, (u + AHEAD) % RING)
                    if u == 0:
                        sp.wait_ge(pv_done, 5 * i)
                        sp.dma_start(past[:], a["k_past"][i]).then_inc(past_landed, 16)
                        sp.wait_ge(sc_evac, 7 * i)
                        sp.dma_start(g_b[:], g_dram[bass.ds(i, 1), :].to_broadcast([P, GW])).then_inc(g_landed, 16)
                    if u == 6:
                        sp.wait_ge(qkn_ready, 2 * i + 2)
                        sp.dma_start(o["k"][i], kn[:]).then_inc(k_stored, 16)
                    if u == 7:
                        sp.wait_ge(tile_evac, 8 * i + 4)
                        sp.dma_start(o["v"][i], vf[:]).then_inc(v_stored, 16)
                    if u == 11:
                        sp.wait_ge(conv_done, 2 * (i + 1))
                        sp.dma_start(conv_w[:], a["conv_w"][i]).then_inc(cw_landed, 16)
                        sp.dma_start(ext[:, S_ST:S_U], a["state"][i]).then_inc(cw_landed, 16)
                    if u == 12:
                        sp.wait_ge(sc_done, 7 * i + 6)
                        sp.dma_start(past[:], a["v_past"][i]).then_inc(past_landed, 16)
                    if u == 14:
                        sp.wait_ge(u_ready, 2 * (i + 1))
                        sp.dma_start(o["conv_p"][i], ext[:, NP:NP + PADW]).then_inc(c_stored, 16)
                        sp.dma_start(o["conv_s"][i], ext[:, EXT - PADW:EXT]).then_inc(c_stored, 16)
                    if u == 15:
                        sp.wait_ge(tile_evac, 8 * i + 8)
                        sp.dma_start(gb_dram[i], s_gb[:]).then_inc(gb_stored, 16)
                sp.wait_ge(tile_evac, 8 * i + 9)
                sp.dma_start(m_dram[i], s_m[:]).then_inc(m_stored, 16)

            sp.wait_ge(gb_stored, 16 * H)

            def b_turn(t):
                for u in range(4):
                    sp.wait_ge(lo_ready, B0 + 4 * t + u + AHEAD - RING + 1)
                    load_unit(B0 + 4 * t + u + AHEAD, (u + AHEAD) % RING)
                    if u % 2:
                        sp.wait_ge(tile_evac, 8 * H + 2 * t + u // 2 + 2)
                        sp.dma_start(m_dram[2 * t + H + u // 2], s_m[:]).then_inc(m_stored, 16)

            with sp.Fori(0, 7) as t:
                b_turn(t)
            with sp.Fori(0, 4) as t:
                for r in range(2):
                    sp.wait_ge(yb_ready, 2 * t)
                    sp.dma_start(gb_in[:, r], gb_dram[2 * t + r]).then_inc(gb_landed[r], 16)
                b_turn(t + 7)
            b_turn(11)

            sp.wait_ge(m_stored, 16 * 2 * KT)
            sp.wait_ge(yb_lo_ready, H)
            with sp.Fori(0, KT // 2) as t:
                for r in range(2):
                    sp.wait_ge(merged, 2 * t)
                    sp.dma_start(m_in[:, r, 0], m_dram[2 * t + r]).then_inc(m_landed[r], 16)
                    sp.dma_start(m_in[:, r, 1], m_dram[2 * t + r + KT]).then_inc(m_landed[r], 16)
                    for g in range(2):
                        sp.wait_ge(gate_used, 4 * t + 2 * r)
                        sp.dma_start(w_gate[:, g], a["w_gate"][4 * t + 2 * r + g]).then_inc(gate_landed[g], 16)
                    for u in (2 * r, 2 * r + 1):
                        sp.wait_ge(lo_ready, C0 + 4 * t + u + AHEAD - RING + 1)
                        load_unit(C0 + 4 * t + u + AHEAD, (u + AHEAD) % RING)

            sp.wait_ge(merged, KT)
            def x_ahead(t):
                for r in range(2):
                    sp.wait_ge(y_ready, 6 * t)
                    sp.dma_start(x_in[:, r], a["xt"][2 * t + r]).then_inc(xin_landed[r], 16)

            def store_y(t):
                for r in range(2):
                    sp.wait_ge(y_ready, 6 * t + 3 * r + 3)
                    sp.dma_start(o["y"][2 * t + r], y_out[:, r]).then_inc(y_stored[r], 16)

            with sp.Fori(0, 6) as t:
                x_ahead(t)
                for u in range(4):
                    sp.wait_ge(lo_ready, D0 + 4 * t + u + AHEAD - RING + 1)
                    load_unit(D0 + 4 * t + u + AHEAD, (u + AHEAD) % RING)
                store_y(t)
            sp.wait_ge(lo_ready, N_UNITS - RING)
            load_unit(N_UNITS - 1, (N_UNITS - 1) % RING)
            with sp.Fori(6, 8) as t:
                x_ahead(t)
                store_y(t)
            for s, n in ((logf_stored, 2), (k_stored, H), (v_stored, H), (c_stored, 2 * H),
                         (y_stored[0], KT // 2), (y_stored[1], KT // 2)):
                sp.wait_ge(s, 16 * n)

        @block.gpsimd
        def _(pool):
            pool.memset(ones[:], 1.0).then_inc(pool_step, 1)
            pool.memset(eps_c[:], EPS).then_inc(pool_step, 1)
            pool.memset(ident[:], 0.0).then_inc(pool_step, 1)
            pool.memset(causal[:], 0.0).then_inc(pool_step, 1)
            pool.memset(ch_sum[:], 0.0).then_inc(pool_step, 1)
            pool.wait_ge(pool_step, 5)
            pool.affine_select(out=ident[:], in_=ident[:], compare_op=ALU.not_equal, fill=1.0, base=0,
                               pattern=[[-1, P]], channel_multiplier=1).then_inc(masks_ready, 1)
            pool.affine_select(out=upto[:], in_=ones[:], compare_op=ALU.is_ge, fill=0.0, base=0,
                               pattern=[[1, P]], channel_multiplier=-1).then_inc(masks_ready, 1)
            pool.affine_select(out=after[:], in_=ones[:], compare_op=ALU.is_gt, fill=0.0, base=0,
                               pattern=[[-1, P]], channel_multiplier=1).then_inc(masks_ready, 1)
            pool.affine_select(out=causal[:], in_=causal[:], compare_op=ALU.is_ge, fill=MASKED, base=0,
                               pattern=[[-1, P]], channel_multiplier=1).then_inc(masks_ready, 1)
            with pool.Fori(0, H + 1) as i:
                pool.wait_ge(conv_done, 2 * (i + 1))
                pool.wait_ge(summed, i)
                pool.tensor_tensor(ch_sum[:], ch_sum[:], cv[:, i], ALU.add).then_inc(summed, 1)
            pool.wait_ge(centred, 1)
            pool.memset(sq_sum[:], 0.0).then_inc(sq_summed, 1)
            with pool.Fori(0, H) as i:
                pool.wait_ge(sqb_ready, i + 1)
                pool.wait_ge(sq_summed, i + 1)
                pool.tensor_tensor(sq_sum[:], sq_sum[:], sq_b[:], ALU.add).then_inc(sq_summed, 1)

        @block.scalar
        def _(act):
            act.wait_ge(const_in, 16 * 8)
            act.activation(c_silu[:], c_in[:], ACT.Silu).then_inc(silu_c, 1)
            for k in range(KT):
                if k % 4 == 0:
                    act.wait_ge(x_landed, 16 * 4)
                if k >= 4:
                    act.wait_ge(sqx_used, k - 3)
                act.activation(sq_x[:, k % 4], x_t[:, k], ACT.Square).then_inc(sqx_ready, 1)
            act.wait_ge(sqx_used, KT)
            act.wait_ge(masks_ready, 1)
            act.activation(halves(rstd_x[:]), banks(X), ACT.Sqrt, scale=1.0 / D, bias=eps_c[:]).then_inc(rstdx_ready, 1)
            with act.Fori(0, KT) as k:
                act.wait_ge(h_ready, 2 * k + 2)
                act.activation(h_hi[:, k], x_t[:, k], ACT.Copy).then_inc(h_hi_ready, 1)
            act.activation(w_f_hi[:], w_f[:], ACT.Copy).then_inc(wf_hi_ready, 1)

            def hi(n, slot, use, prior=None):
                act.wait_ge(w_landed[slot], use)
                if prior is not None:
                    act.wait_ge(w_used, prior)
                act.activation(w_hi[:, slot], w_raw[:, slot], ACT.Copy).then_inc(hi_ready, 1)

            for n in range(LEAD):
                hi(n, n, uses(0))
            act.wait_ge(tile_evac, 1)
            act.activation(e_f[:], z_f[:], ACT.Abs).then_inc(f_act, 1)
            act.wait_ge(f_act, 1)
            act.activation(e_f[:], e_f[:], ACT.Exp, scale=-1.0).then_inc(f_act, 1)
            act.wait_ge(f_act, 2)
            act.activation(e_f[:], e_f[:], ACT.Ln, bias=ones[:, 0:1]).then_inc(f_act, 1)

            act.wait_ge(g_stored, 16)
            with act.Fori(0, H) as i:
                def evac(t, dst, func):
                    return act.activation(dst, banks(2 * (t % 2)), func)

                def norm_root(n, bank):
                    act.wait_ge(ss_done, 2 * i + n + 1)
                    act.wait_ge(qkn_ready, 2 * i + n)
                    act.activation(halves(rs[:]), banks(bank), ACT.Sqrt, scale=1.0 / P, bias=eps_c[:]).then_inc(std_ready, 1)

                def exp(j):
                    act.wait_ge(prep_done, 5 * i + j + 1)
                    s = s_p[:, j % 2, 0:P * (j + 1)] if j < QB else s_s[0:NS]
                    m = P if j < QB else NS
                    act.activation(s, s, ACT.Exp, bias=stat_neg[0:m, j:j + 1], accum_out=stat_sum[0:m, j:j + 1]).then_inc(exp_done, 1)

                def probs_t(j):
                    act.wait_ge(tr_done, 5 * i + j + 1)
                    act.activation(p_t[:, 0:j + 1].rearrange("p j q -> p (j q)"), ps[:, Z, 0:P * (j + 1)], ACT.Copy).then_inc(pt_ready, 1)

                for u in range(A_STEPS):
                    hi(None, (u + LEAD) % RING, uses(4 * i + (u + LEAD) // RING), A_STEPS * i + u)
                    if u == 2:
                        evac(0, halves(qn[:]), ACT.Copy).then_inc(tile_evac, 1)
                        act.wait_ge(tile_evac, 8 * i + 2)
                        act.activation(sq[:], qn[:], ACT.Square).then_inc(sq_ready, 1)
                    if u == 3:
                        norm_root(0, X)
                    if u == 4:
                        act.wait_ge(k_stored, 16 * i)
                        evac(1, halves(kn[:]), ACT.Copy).then_inc(tile_evac, 1)
                        act.wait_ge(tile_evac, 8 * i + 3)
                        act.activation(sq[:], kn[:], ACT.Square).then_inc(sq_ready, 1)
                    if u == 5:
                        norm_root(1, Z)
                    if u == 6:
                        act.wait_ge(v_stored, 16 * i)
                        evac(2, halves(vf[:]), ACT.Copy).then_inc(tile_evac, 1)
                    if u == 7:
                        act.wait_ge(vt_done, i + 1)
                        act.wait_ge(pv_done, 5 * i)
                        act.activation(v_tok[:, 0:QB].rearrange("p j d -> p (j d)"), ps[:, Z, :], ACT.Copy).then_inc(vtok_ready, 1)
                        act.activation(v_tok[0:NS, QB], ps[0:NS, V, 0:P], ACT.Copy).then_inc(vtok_ready, 1)
                        exp(0)
                    if u == 8:
                        evac(3, halves(y_a[:, i]), ACT.Silu).then_inc(tile_evac, 1)
                        exp(1)
                    if u == 9:
                        probs_t(0)
                        exp(2)
                    if u == 10:
                        act.wait_ge(conv_done, 2 * (i + 1))
                        act.wait_ge(c_stored, 32 * i)
                        act.activation(ext[:, PADW:PADW + HC], ps[:, 0, 0:HC], ACT.Copy)
                        act.activation(ext[:, PADW + HC:S_ST], ps[:, 1, 0:NP - HC], ACT.Copy)
                        act.activation(ext[:, S_U:EXT], ps[:, 1, NP - HC:HC], ACT.Copy).then_inc(tile_evac, 1)
                        probs_t(1)
                        exp(3)
                    if u == 11:
                        probs_t(2)
                    if u == 12:
                        evac(5, halves(sig[:]), ACT.Sigmoid).then_inc(tile_evac, 1)
                        probs_t(3)
                    if u == 13:
                        exp(4)
                    if u == 14:
                        act.wait_ge(gb_stored, 16 * i)
                        evac(6, halves(s_gb[:]), ACT.Silu).then_inc(tile_evac, 1)
                    if u == 15:
                        act.wait_ge(tr_done, 5 * i + 5)
                        act.activation(ps_t[:].rearrange("p j q -> p (j q)"), ps[:, Z, :], ACT.Copy).then_inc(pt_ready, 1)
                        act.activation(pn_t[:], ps[0:NS, X, 0:NS], ACT.Copy).then_inc(pt_ready, 1)
                act.wait_ge(w_used, A_STEPS * i + 16)
                act.wait_ge(m_stored, 16 * i)
                evac(7, halves(s_m[:]), ACT.Sigmoid).then_inc(tile_evac, 1)

            def b_turn(t, work=lambda r: None):
                for r in range(2):
                    for u in (2 * r, 2 * r + 1):
                        hi(None, (u + LEAD) % RING, uses(B0 // 4 + t + (u + LEAD) // RING), B0 + 4 * t + u)
                    work(r)
                    act.wait_ge(w_used, B0 + 4 * t + 2 * r + 2)
                    act.wait_ge(m_stored, 16 * (H + 2 * t + r))
                    act.activation(halves(s_m[:]), banks(2 * r), ACT.Sigmoid).then_inc(tile_evac, 1)

            with act.Fori(0, 2) as t:
                b_turn(t)
            act.wait_ge(pv_evac, 5 * H)
            act.wait_ge(k_stored, 16 * H)
            act.wait_ge(v_stored, 16 * H)
            act.wait_ge(gb_stored, 16 * H)
            act.wait_ge(conv_done, 2 * (H + 1))
            with act.Fori(2, 6) as t:
                def squares(r):
                    c = 2 * (t - 2) + r
                    act.activation(ya_hi[:, c], y_a[:, c], ACT.Copy).then_inc(ya_hi_ready, 1)
                    act.wait_ge(centred, c + 2)
                    act.wait_ge(sq_summed, c + 1)
                    act.activation(sq_b[:], cv[:, c + 1], ACT.Square).then_inc(sqb_ready, 1)
                b_turn(t, squares)
            b_turn(6)
            act.wait_ge(var_done, 1)
            act.activation(halves(rstd[:]), banks(X), ACT.Sqrt, scale=1.0 / (H * P), bias=eps_c[:]).then_inc(rstd_ready, 1)
            with act.Fori(7, 11) as t:
                def silus(r):
                    c = 2 * (t - 7) + r
                    act.wait_ge(scaled, c + 1)
                    act.activation(cv[:, c + 1], cv[:, c + 1], ACT.Silu, scale=ln_cur[:, 0:1], bias=ln_cur[:, 1:2]).then_inc(ln_silu, 1)
                b_turn(t, silus)
            b_turn(11)
            with act.Fori(0, H) as c:
                act.activation(yb_hi[:, c], cv[:, c + 1], ACT.Copy).then_inc(yb_hi_ready, 1)

            with act.Fori(0, KT // 2) as t:
                for r in range(2):
                    for u in (2 * r, 2 * r + 1):
                        hi(None, (u + LEAD) % RING, uses(C0 // 4 + t + (u + LEAD) // RING), C0 + 4 * t + u)
                    act.wait_ge(merged, 2 * t + r + 1)
                    act.activation(mg_hi[:, 2 * t + r], merge[:], ACT.Copy).then_inc(mg_hi_ready, 1)

            with act.Fori(0, N_D // 4 - 1) as t:
                for u in range(4):
                    hi(None, (u + LEAD) % RING, uses(D0 // 4 + t + (u + LEAD) // RING), D0 + 4 * t + u)
            hi(None, RING - 1, uses(N_UNITS // 4 - 1), N_UNITS - 4)

        @block.vector
        def _(dve):
            base, turn, per, k = [0], [None], [0], [0]

            def step(ins):
                ins.then_inc(chain, 1)
                k[0] += 1
                dve.wait_ge(chain, base[0] + k[0] if turn[0] is None else turn[0] * per[0] + base[0] + k[0])

            def enter(i, n):
                base[0], k[0] = base[0] + k[0], 0
                turn[0], per[0] = i, n

            def leave(turns, first=0):
                assert k[0] == per[0], (k[0], per[0])
                base[0], k[0], turn[0] = base[0] + turns * per[0], 0, None

            dve.memset(ext[:], 0.0).then_inc(zeroed, 1)
            dve.memset(conv_w[:], 0.0).then_inc(zeroed, 1)
            dve.wait_ge(rstdx_ready, 1)
            step(dve.reciprocal(rstd_x[:], rstd_x[:]))
            with dve.Fori(0, KT) as i:
                dve.tensor_tensor(x_t[:, i], x_t[:, i], rstd_x[:], ALU.mult).then_inc(xn_ready, 1)

            with dve.Fori(0, KT // 2) as i:
                enter(i, 2)
                for r in range(2):
                    m = 4 * i + 2 * r
                    dve.wait_ge(ada_used, 2 * (m + 1))
                    dve.tensor_scalar(mod[:, m], ps[:, 2 * r, 0:2], b_ada[:, bass.ds(m, 1)], None, ALU.add).then_inc(mod_ready, 1)
                    dve.wait_ge(ada_used, 2 * (m + 2))
                    step(dve.tensor_scalar(mod[:, m + 1], ps[:, 2 * r + 1, 0:2], b_ada[:, bass.ds(m + 1, 1)], 1.0, ALU.add, ALU.add))
                    kt = 2 * i + r
                    dve.tensor_scalar(mod[:, m + 1], mod[:, m + 1], norm_g[:, bass.ds(kt, 1)], None, ALU.mult).then_inc(mod_ready, 1)
                    dve.wait_ge(mod_ready, m + 2)
                    dve.wait_ge(xn_ready, kt + 1)
                    for lo, hi_, s in ((0, NP, 0), (NP, T, 1)):
                        dve.tensor_scalar(x_t[:, kt, lo:hi_], x_t[:, kt, lo:hi_], mod[:, m + 1, s:s + 1],
                                          mod[:, m, s:s + 1], ALU.mult, ALU.add).then_inc(h_ready, 1)
                for r in range(2):
                    kt = 2 * i + r
                    dve.wait_ge(h_hi_ready, kt + 1)
                    dve.tensor_tensor(h_lo[:, kt], x_t[:, kt], h_hi[:, kt].bitcast(F32), ALU.subtract).then_inc(h_lo_ready, 1)
                leave(KT // 2)
            dve.wait_ge(wf_hi_ready, 1)
            dve.tensor_tensor(w_f_lo[:], w_f[:], w_f_hi[:].bitcast(F32), ALU.subtract).then_inc(wf_lo_ready, 1)

            def lo(ready, slot):
                dve.wait_ge(hi_ready, ready)
                dve.tensor_tensor(w_lo[:, slot], w_raw[:, slot], w_hi[:, slot].bitcast(F32), ALU.subtract).then_inc(lo_ready, 1)

            for n in range(LEAD):
                lo(n + 1, n)
            dve.wait_ge(f_done, 1)
            dve.tensor_tensor(z_f[:], ps[:, 0, 0:5 * H].rearrange("p (t h) -> p t h", h=H), b_f[:], ALU.add).then_inc(tile_evac, 1)
            dve.wait_ge(f_act, 3)
            dve.scalar_tensor_tensor(out=logf[:], in0=z_f[:], scalar=0.0, in1=e_f[:], op0=ALU.min, op1=ALU.subtract).then_inc(logf_ready, 1)
            dve.wait_ge(g_done, 1)
            for bank, at, n, sign in ((X, 0, NP, -1.0), (Y, G_PAST, 512, 1.0), (Z, G_PAST + 512, 512, 1.0), (V, G_NEW, NS, -1.0)):
                dve.tensor_scalar(g_rows[:, at:at + n], ps[0:H, bank, 0:n], sign, None, ALU.mult).then_inc(g_rows_ready, 1)
            dve.wait_ge(g_stored, 16)

            def conv_step(taps, out):
                for w in taps:
                    if w == 0:
                        step(dve.tensor_scalar(acc[:], ext[:, 0:ACCW], conv_w[:, 0:1], conv_w[:, W:W + 1], ALU.mult, ALU.add))
                    elif w < W - 1:
                        step(dve.scalar_tensor_tensor(out=acc[:], in0=ext[:, w:w + ACCW], scalar=conv_w[:, w:w + 1],
                                                      in1=acc[:], op0=ALU.mult, op1=ALU.add))
                    else:
                        for a0, n, c0 in ((0, NP, 0), (S_ST, NS, NP)):
                            dve.scalar_tensor_tensor(out=out[:, c0:c0 + n], in0=ext[:, w + a0:w + a0 + n],
                                                     scalar=conv_w[:, w:w + 1], in1=acc[:, a0:a0 + n],
                                                     op0=ALU.mult, op1=ALU.add).then_inc(conv_done, 1)

            CONV = [range(0, 4)] + [range(4 + 3 * j, 7 + 3 * j) for j in range(9)]
            CONV_STEPS = W - 1
            dve.memset(s_s[NS:P, 0:P], 0.0).then_inc(zeroed, 1)
            dve.wait_ge(zeroed, 3)

            with dve.Fori(0, H) as i:
                enter(i, CONV_STEPS + 2 + 2 * 5)

                def normed(n, dst):
                    dve.wait_ge(std_ready, 2 * i + n + 1)
                    step(dve.reciprocal(rs[:], rs[:]))
                    dve.scalar_tensor_tensor(out=dst[:], in0=dst[:], scalar=qk_g[:, n:n + 1], in1=rs[:],
                                             op0=ALU.mult, op1=ALU.mult).then_inc(qkn_ready, 1)

                def scores_in(n, dst, bank, bias):
                    dve.wait_ge(sc_done, 7 * i + n + 1)
                    m, w = dst.shape[0], dst.shape[1]
                    dve.scalar_tensor_tensor(out=dst, in0=ps[0:m, bank, 0:w], scalar=SCALE, in1=g_b[0:m, bias:bias + w],
                                             op0=ALU.mult, op1=ALU.add).then_inc(sc_evac, 1)

                def prepare(j, n, s, last, m):
                    dve.wait_ge(sc_evac, 7 * i + n + 1)
                    step(dve.tensor_tensor(s[:, last:last + m], s[:, last:last + m], causal[0:m, 0:m], ALU.add))
                    step(dve.tensor_reduce(stat_max[0:m, j:j + 1], s[:, 0:last + m], AX.X, ALU.max))
                    dve.tensor_scalar(stat_neg[0:m, j:j + 1], stat_max[0:m, j:j + 1], -1.0, None, ALU.mult).then_inc(prep_done, 1)

                def normalise(j, s, m):
                    dve.wait_ge(exp_done, 5 * i + j + 1)
                    dve.reciprocal(stat_inv[0:m, j:j + 1], stat_sum[0:m, j:j + 1]).then_inc(inv_done, 1)
                    dve.wait_ge(inv_done, 5 * i + j + 1)
                    dve.tensor_scalar(s, s, stat_inv[0:m, j:j + 1], None, ALU.mult).then_inc(p_ready, 1)

                def attended(j):
                    dve.wait_ge(pv_done, 5 * i + j + 1)
                    n = P if j < QB else NS
                    y = y_a[:, i, P * j:P * j + n]
                    dve.tensor_tensor(y, y, ps[:, V, 0:n], ALU.mult).then_inc(pv_evac, 1)

                for u in range(A_STEPS):
                    lo(A_STEPS * i + u + LEAD + 1, (u + LEAD) % RING)
                    if u == 0:
                        dve.wait_ge(u_ready, 2 * i)
                        dve.wait_ge(cw_landed, 32 * i)
                    if u == 3:
                        normed(0, qn)
                    if u == 5:
                        normed(1, kn)
                    if u == 7:
                        dve.wait_ge(g_landed, 16 * (i + 1))
                    if 8 <= u < 12:
                        normalise(u - 8, s_p[:, u % 2, 0:P * (u - 7)], P)
                    if 7 <= u < 11:
                        b = u - 7
                        scores_in(b, s_p[:, b % 2, 0:P * (b + 1)], X + b % 2, 0)
                        prepare(b, b, s_p[:, b % 2], P * b, P)
                    if u == 10:
                        dve.wait_ge(tile_evac, 8 * i + 5)
                    if 10 <= u < 14:
                        attended(u - 10)
                    if u == 11:
                        scores_in(4, s_s[0:NS, 0:512], X, G_PAST)
                    if u == 12:
                        scores_in(5, s_s[0:NS, 512:1024], Y, G_PAST + 512)
                        dve.wait_ge(tile_evac, 8 * i + 7)
                        dve.tensor_tensor(ext[:, PADW:S_ST], ext[:, PADW:S_ST], sig[:, 0:NP], ALU.mult).then_inc(u_ready, 1)
                        dve.tensor_tensor(ext[:, S_U:EXT], ext[:, S_U:EXT], sig[:, NP:T], ALU.mult).then_inc(u_ready, 1)
                    if u == 13:
                        scores_in(6, s_s[0:NS, PAST:PAST + NS], X, G_NEW)
                        prepare(4, 6, s_s[0:NS], PAST, NS)
                    if u == 14:
                        normalise(4, s_s[0:NS], NS)
                    if u < 10:
                        conv_step(CONV[u], cv[:, i])
                attended(4)
                leave(H)

            def b_los(t, work=lambda r: None):
                for r in range(2):
                    for u in (2 * r, 2 * r + 1):
                        lo(B0 + 4 * t + u + LEAD + 1, (u + LEAD) % RING)
                    work(r)

            dve.wait_ge(u_ready, 2 * H)
            dve.wait_ge(cw_landed, 32 * H)
            conv_of = [range(0, 8), range(8, 16), range(16, 24), range(24, 31)]
            b_los(0, lambda r: conv_step(conv_of[r], cv[:, H]))
            b_los(1, lambda r: conv_step(conv_of[2 + r], cv[:, H]))
            dve.wait_ge(mean_done, 1)
            dve.wait_ge(k_stored, 16 * H)
            dve.wait_ge(v_stored, 16 * H)
            dve.wait_ge(gb_stored, 16 * H)
            dve.wait_ge(c_stored, 32 * H)
            dve.tensor_scalar(halves(mu[:]), banks(X), 1.0 / (H * P), None, ALU.mult).then_inc(centred, 1)
            dve.wait_ge(centred, 1)
            with dve.Fori(2, 6) as t:
                def centre(r):
                    c = 2 * (t - 2) + r
                    dve.tensor_tensor(cv[:, c + 1], cv[:, c + 1], mu[:], ALU.subtract).then_inc(centred, 1)
                    dve.wait_ge(ya_hi_ready, c + 1)
                    dve.tensor_tensor(ya_lo[:, c], y_a[:, c], ya_hi[:, c].bitcast(F32), ALU.subtract).then_inc(ya_lo_ready, 1)
                b_los(t, centre)
            b_los(6)
            dve.wait_ge(rstd_ready, 1)
            step(dve.reciprocal(rstd[:], rstd[:]))
            with dve.Fori(7, 11) as t:
                def scale_c(r):
                    c = 2 * (t - 7) + r
                    dve.tensor_copy(ln_cur[:], ln_gb[:, c]).then_inc(lncur_ready, 1)
                    dve.wait_ge(lncur_ready, c + 1)
                    dve.tensor_tensor(cv[:, c + 1], cv[:, c + 1], rstd[:], ALU.mult).then_inc(scaled, 1)
                    dve.wait_ge(ln_silu, c + 1)
                    dve.wait_ge(gb_landed[r], 16 * (t - 6))
                    dve.tensor_tensor(cv[:, c + 1], cv[:, c + 1], gb_in[:, r], ALU.mult).then_inc(yb_ready, 1)
                b_los(t, scale_c)
            b_los(11)
            with dve.Fori(0, H) as c:
                dve.wait_ge(yb_hi_ready, c + 1)
                dve.tensor_tensor(yb_lo[:, c], cv[:, c + 1], yb_hi[:, c].bitcast(F32), ALU.subtract).then_inc(yb_lo_ready, 1)

            with dve.Fori(0, KT // 2) as t:
                enter(t, 2)
                for r in range(2):
                    for u in (2 * r, 2 * r + 1):
                        lo(C0 + 4 * t + u + LEAD + 1, (u + LEAD) % RING)
                    j = 2 * t + r
                    bank = 4 * r
                    dve.wait_ge(w_used, C0 + 4 * t + 2 * r + 2)
                    dve.tensor_scalar(gate[:, j], ps[:, bank, HC + 12:HC + 14], b_ada[:, bass.ds(j + 2 * KT, 1)], None,
                                      ALU.add).then_inc(gate_ready, 1)
                    dve.wait_ge(m_landed[r], 32 * (t + 1))
                    dve.wait_ge(mg_lo_ready, j)
                    dve.tensor_tensor(halves(merge[:]), banks(bank), halves(m_in[:, r, 0]), ALU.mult).then_inc(c_evac, 1)
                    step(dve.tensor_tensor(halves(merge_b[:]), banks(bank + 2), halves(m_in[:, r, 1]), ALU.mult))
                    dve.wait_ge(c_evac, j + 1)
                    dve.tensor_tensor(merge[:], merge[:], merge_b[:], ALU.add).then_inc(merged, 1)
                    dve.wait_ge(mg_hi_ready, j + 1)
                    dve.tensor_tensor(mg_lo[:, j], merge[:], mg_hi[:, j].bitcast(F32), ALU.subtract).then_inc(mg_lo_ready, 1)
                leave(KT // 2)

            def out_tile(t, r):
                j = 2 * t + r
                dve.wait_ge(w_used, D0 + 4 * t + 2 * r + 2)
                dve.wait_ge(xin_landed[r], 16 * (t + 1))
                dve.wait_ge(y_stored[r], 16 * t)
                for bank, lo_, hi_, at, s in ((0, 0, HC, 0, 0), (1, 0, NP - HC, HC, 0), (1, NP - HC, HC, NP, 1)):
                    n = hi_ - lo_
                    dve.scalar_tensor_tensor(out=y_out[:, r, at:at + n], in0=ps[:, 2 * r + bank, lo_:hi_],
                                             scalar=gate[:, j, s:s + 1], in1=x_in[:, r, at:at + n],
                                             op0=ALU.mult, op1=ALU.add).then_inc(y_ready, 1)

            dve.wait_ge(gate_ready, KT)
            with dve.Fori(0, N_D // 4 - 1) as t:
                for r in range(2):
                    for u in (2 * r, 2 * r + 1):
                        lo(D0 + 4 * t + u + LEAD + 1, (u + LEAD) % RING)
                    out_tile(t, r)
            lo(N_UNITS, RING - 1)
            for r in range(2):
                out_tile(N_D // 4 - 1, r)

        @block.tensor
        def _(pe):
            pe.wait_ge(masks_ready, 4)
            for k in range(KT):
                pe.wait_ge(sqx_ready, k + 1)
                for c in range(2):
                    mm = pe.matmul(ps[:, X + c, 0:HC], ones[:], sq_x[:, k % 4, c * HC:(c + 1) * HC], start=(k == 0), stop=(k == KT - 1))
                mm.then_inc(sqx_used, 1)
            pe.wait_ge(silu_c, 1)
            with pe.Fori(0, KT // 2) as i:
                for m in range(4):
                    pe.wait_ge(mod_ready, 4 * i)
                    for half in range(2):
                        slot = (2 * m + half) % RING
                        pe.wait_ge(w_landed[slot], 16 * (2 * i + (2 * m + half) // RING + 1))
                        for kk in range(UK):
                            kt = half * UK + kk
                            mm = pe.matmul(ps[:, m, 0:2], w_raw[:, slot, kk * P:(kk + 1) * P], c_silu[:, kt], start=(kt == 0), stop=(kt == KT - 1))
                        mm.then_inc(ada_used, 1)

            def three(out, w, kk, parts, start, stop):
                (whi, wlo), (xhi, xlo) = w, parts
                n = 0
                for wp, xp in ((whi, xhi), (whi, xlo), (wlo, xhi)):
                    for c in range(2):
                        mm = pe.matmul(out[:, c], wp[:, kk * P:(kk + 1) * P], xp[:, c * HC:(c + 1) * HC],
                                       start=(start and n == 0), stop=(stop and n == 2))
                    n += 1
                return mm

            def unit(ready, slot, bank, src, k0, start, stop):
                pe.wait_ge(hi_ready, ready)
                pe.wait_ge(lo_ready, ready)
                for kk in range(UK):
                    mm = three(banks(bank), (w_hi[:, slot], w_lo[:, slot]), kk, (src[0][:, k0 + kk], src[1][:, k0 + kk]),
                               start and kk == 0, stop and kk == UK - 1)
                mm.then_inc(w_used, 1)

            pe.wait_ge(h_lo_ready, KT)
            pe.wait_ge(wf_lo_ready, 1)
            pe.wait_ge(mod_ready, 2 * KT)
            for tt in range(5):
                at = P * tt if tt < QB else T - P
                for k in range(KT):
                    for n, (x_, w_) in enumerate(((h_hi, w_f_hi), (h_lo, w_f_hi), (h_hi, w_f_lo))):
                        mm = pe.matmul(ps[:, 0, H * tt:H * (tt + 1)], x_[:, k, at:at + P], w_[:, k],
                                       start=(k == 0 and n == 0), stop=(k == KT - 1 and n == 2))
            mm.then_inc(f_done, 1)
            pe.wait_ge(logf_ready, 1)
            for tt in range(QB):
                for t2 in range(tt + 1):
                    pe.matmul(ps[0:H, X, P * tt:P * (tt + 1)], logf[:, t2], ones[:] if t2 < tt else upto[:], start=(t2 == 0), stop=(t2 == tt))
            for tt in range(CT):
                for t2 in range(tt, CT):
                    pe.matmul(ps[0:H, Y + tt // 4, P * (tt % 4):P * (tt % 4 + 1)], logf_past[:, t2], ones[:] if t2 > tt else after[:],
                              start=(t2 == tt), stop=(t2 == CT - 1))
            pe.matmul(ps[0:H, V, 0:NS], logf[NS:P, QB], upto[NS:P, NS:P], start=True, stop=True).then_inc(g_done, 1)
            pe.wait_ge(g_rows_ready, 4)

            h_parts = (h_hi, h_lo)
            with pe.Fori(0, H) as i:
                def square_sum(n, bank):
                    pe.wait_ge(sq_ready, 2 * i + n + 1)
                    for c in range(2):
                        mm = pe.matmul(ps[:, bank + c, 0:HC], ones[:], sq[:, c * HC:(c + 1) * HC], start=True, stop=True)
                    mm.then_inc(ss_done, 1)

                def scores(n, bank, q, keys, evacuated):
                    pe.wait_ge(sc_evac, 7 * i + evacuated)
                    pe.matmul(ps[0:q.shape[1], bank, 0:keys.shape[1]], q, keys, start=True, stop=True).then_inc(sc_done, 1)

                def prompt_scores(b):
                    scores(b, X + b % 2, qn[:, P * b:P * (b + 1)], kn[:, 0:P * (b + 1)], max(b - 1, 0))

                def turn_probs(b):
                    pe.wait_ge(p_ready, 5 * i + b + 1)
                    if b:
                        pe.wait_ge(pt_ready, 6 * i + b)
                    for j in range(b + 1):
                        mm = pe.transpose(ps[:, Z, P * j:P * (j + 1)], s_p[:, b % 2, P * j:P * (j + 1)], ident[:])
                    mm.then_inc(tr_done, 1)

                def values(b):
                    pe.wait_ge(pt_ready, 6 * i + b + 1)
                    pe.wait_ge(pv_evac, 5 * i + b)
                    for j in range(b + 1):
                        mm = pe.matmul(ps[:, V, 0:P], v_tok[:, j], p_t[:, j], start=(j == 0), stop=(j == b))
                    mm.then_inc(pv_done, 1)

                for u in range(A_STEPS):
                    t, half = divmod(u, 2)
                    if half == 0:
                        pe.wait_ge(tile_evac, 8 * i + t)
                    unit(A_STEPS * i + u + 1, u % RING, 2 * (t % 2), h_parts, UK * half, half == 0, half == 1)
                    if u == 2:
                        pe.wait_ge(pv_evac, 5 * i)
                        square_sum(0, X)
                    if u == 4:
                        square_sum(1, Z)
                    if u == 6:
                        pe.wait_ge(tile_evac, 8 * i + 4)
                        pe.wait_ge(std_ready, 2 * i + 2)
                        for j in range(QB):
                            pe.transpose(ps[:, Z, P * j:P * (j + 1)], vf[:, P * j:P * (j + 1)], ident[:])
                        pe.transpose(ps[0:NS, V, 0:P], vf[:, NP:T], ident[:]).then_inc(vt_done, 1)
                        pe.wait_ge(qkn_ready, 2 * i + 2)
                        prompt_scores(0)
                    if u == 7:
                        prompt_scores(1)
                    if u == 8:
                        pe.wait_ge(vtok_ready, 2 * i + 2)
                        turn_probs(0)
                        prompt_scores(2)
                    if 9 <= u < 13:
                        values(u - 9)
                        if u < 12:
                            turn_probs(u - 8)
                    if u == 9:
                        prompt_scores(3)
                    if u == 10:
                        pe.wait_ge(past_landed, 32 * i + 16)
                        scores(4, X, qn[:, NP:T], past[:, 0:512], 3)
                    if u == 11:
                        scores(5, Y, qn[:, NP:T], past[:, 512:1024], 4)
                    if u == 12:
                        scores(6, X, qn[:, NP:T], kn[:, NP:T], 5)
                    if u == 14:
                        pe.wait_ge(p_ready, 5 * i + 5)
                        pe.wait_ge(pt_ready, 6 * i + 4)
                        pe.transpose(ps[:, Z, 0:P], s_s[:, 0:P], ident[:])
                        for j in range(1, CT):
                            pe.transpose(ps[:, Z, NS * j:NS * (j + 1)], s_s[0:NS, P * j:P * (j + 1)], ident[0:NS, 0:NS])
                        pe.transpose(ps[0:NS, X, 0:NS], s_s[0:NS, PAST:PAST + NS], ident[0:NS, 0:NS]).then_inc(tr_done, 1)
                    if u == 15:
                        pe.wait_ge(pt_ready, 6 * i + 6)
                        pe.wait_ge(pv_evac, 5 * i + 4)
                        pe.wait_ge(past_landed, 32 * i + 32)
                        for j in range(CT):
                            pe.matmul(ps[:, V, 0:NS], past[:, P * j:P * (j + 1)], ps_t[:, j], start=(j == 0), stop=False)
                        pe.matmul(ps[:, V, 0:NS], v_tok[0:NS, QB], pn_t[:], start=False, stop=True).then_inc(pv_done, 1)

            def b_turn(t):
                for u in range(4):
                    if u % 2 == 0:
                        pe.wait_ge(tile_evac, 8 * H + 2 * t + u // 2)
                    unit(B0 + 4 * t + u + 1, u, 2 * (u // 2), h_parts, UK * (u % 2), u % 2 == 0, u % 2 == 1)

            def column_sum(src, done):
                for c in range(2):
                    mm = pe.matmul(ps[:, X + c, 0:HC], ones[:], src[:, c * HC:(c + 1) * HC], start=True, stop=True)
                mm.then_inc(done, 1)

            with pe.Fori(0, 2) as t:
                b_turn(t)
            pe.wait_ge(summed, H + 1)
            column_sum(ch_sum, mean_done)
            with pe.Fori(2, 7) as t:
                b_turn(t)
            pe.wait_ge(sq_summed, H + 1)
            column_sum(sq_sum, var_done)
            with pe.Fori(7, B_TURNS) as t:
                b_turn(t)

            pe.wait_ge(tile_evac, 8 * H + 2 * B_TURNS + 1)
            pe.wait_ge(ya_lo_ready, H)
            pe.wait_ge(rstd_ready, 1)
            def merge_turn(t, first=False):
                for r in range(2):
                    if not first:
                        pe.wait_ge(merged, 2 * t + r - 1)
                    for g in range(2):
                        pe.wait_ge(gate_landed[g], 16 * (2 * t + r + 1))
                        for kk in range(UK):
                            kt = g * UK + kk
                            mm = pe.matmul(ps[:, 4 * r, HC + 12:HC + 14], w_gate[:, g, kk * P:(kk + 1) * P], c_silu[:, kt],
                                           start=(kt == 0), stop=(kt == KT - 1))
                        mm.then_inc(gate_used, 1)
                    unit(C0 + 4 * t + 2 * r + 1, 2 * r, 4 * r, (ya_hi, ya_lo), 0, True, True)
                    if first:
                        pe.wait_ge(yb_lo_ready, H)
                    unit(C0 + 4 * t + 2 * r + 2, 2 * r + 1, 4 * r + 2, (yb_hi, yb_lo), 0, True, True)

            merge_turn(0, first=True)
            with pe.Fori(1, KT // 2) as t:
                merge_turn(t)

            def out_turn(t, first=False):
                for r in range(2):
                    if not first:
                        pe.wait_ge(y_ready, 6 * t + 3 * r - 3)
                    for half in range(2):
                        unit(D0 + 4 * t + 2 * r + half + 1, 2 * r + half, 2 * r, (mg_hi, mg_lo), UK * half, half == 0, half == 1)

            pe.wait_ge(mg_lo_ready, KT)
            out_turn(0, first=True)
            with pe.Fori(1, KT // 2) as t:
                out_turn(t)


def kernel(**inp):
    import numpy as np
    import concourse.bacc as bacc
    from concourse.bass_utils import run_bass_kernel_spmd

    def cols(v):
        return v.reshape(-1, P).T

    def units(w):
        kk, nn = w.shape
        return w.reshape(kk // (P * UK), UK, P, nn // P, P).transpose(3, 0, 2, 1, 4).reshape(-1, P, UW)

    x = np.concatenate([inp["x_prompt"][0], inp["x_sample"][0]], 0)
    xt = x.T.reshape(KT, P, T)
    c = np.concatenate([inp["c_prompt"], inp["c_sample"]], 0)
    w_ada, b_ada = inp["w_ada"][0], inp["b_ada"][0]
    n_mod = 2 * KT
    ada_u = units(w_ada)
    order = [t for k in range(KT) for t in (k, KT + k)]
    ada_pairs = ada_u.reshape(3 * KT, 2, P, UW)
    b_cols = cols(b_ada)

    w_in = inp["w_in"][0]
    DA = H * P
    parts, at = {}, 0
    for name, n in (("q", DA), ("k", DA), ("v", DA), ("f", H), ("ga", DA), ("gl", DA), ("gg", DA), ("gb", DA), ("ma", D), ("mb", D)):
        parts[name] = w_in[:, at:at + n]
        at += n
    u = {n: units(p).reshape(-1, 2, P, UW) for n, p in parts.items() if n != "f"}
    turns = np.stack([u[n][:H] for n in ("q", "k", "v", "ga", "gl", "gg", "gb", "ma")], 1).reshape(-1, P, UW)
    rest = np.concatenate([u["ma"][H:], u["mb"]], 0).reshape(-1, P, UW)
    w_o = np.stack([units(inp["w_oa"][0]), units(inp["w_ob"][0])], 1).reshape(-1, P, UW)
    stream = np.concatenate([turns, rest, w_o, units(inp["w_out"][0])], 0)

    arrays = {
        "x": xt.transpose(1, 0, 2),
        "xt": xt,
        "c": c.T.reshape(KT, P, 2).transpose(1, 0, 2),
        "b_ada": np.concatenate([b_cols[:, order], b_cols[:, n_mod:]], 1),
        "norm_g": cols(inp["norm_g"][0]),
        "qk_g": np.stack([inp["q_norm_g"][0], inp["k_norm_g"][0]], 1),
        "ln_gb": np.stack([cols(inp["conv_ln_g"][0]), cols(inp["conv_ln_b"][0])], 2),
        "w_f": parts["f"].reshape(KT, P, H).transpose(1, 0, 2),
        "b_f": np.broadcast_to(inp["b_f"][0], (P, 5, H)),
        "logf_past": inp["cache_logf"][0, 0].reshape(CT, P, H).transpose(1, 0, 2),
        "w_ada": ada_pairs[order].reshape(-1, P, UW),
        "w_gate": ada_pairs[n_mod:].reshape(-1, P, UW),
        "w": stream,
        "k_past": inp["cache_k"][0, 0].transpose(1, 2, 0),
        "v_past": inp["cache_v"][0, 0].reshape(CT, P, H, P).transpose(2, 1, 0, 3).reshape(H, P, PAST),
        "conv_w": np.concatenate([inp["conv_w"][0].T, inp["conv_b"][0][:, None]], 1).reshape(H, P, W + 1),
        "state": inp["state_conv"][0, 0].T.reshape(H, P, PADW),
    }
    outs = {"y": (KT, P, T), "k": (H, P, T), "v": (H, P, T), "logf_p": (P, QB, H), "logf_s": (NS, H),
            "conv_p": (H, P, PADW), "conv_s": (H, P, PADW)}
    nc = bacc.Bacc("TRN2", target_bir_lowering=False, num_devices=1, dynamic_dma_scratch_size=1024)
    feed, a, o = {}, {}, {}
    for name, v in arrays.items():
        feed[f"in_{name}"] = np.ascontiguousarray(v)
        a[name] = nc.dram_tensor(f"in_{name}", v.shape, F32, kind="ExternalInput").ap()
    for name, shape in outs.items():
        o[name] = nc.dram_tensor(f"out_{name}", shape, F32, kind="ExternalOutput").ap()
    build(nc, a, o)
    r = run_bass_kernel_spmd(nc, [feed], core_ids=[0]).results[0]
    got = {n: np.asarray(r[f"out_{n}"]) for n in outs}

    y = got["y"].reshape(D, T).T
    kv = {n: got[n].transpose(2, 0, 1) for n in ("k", "v")}
    conv = {n: got[n].reshape(DA, PADW).T[None, None] for n in ("conv_p", "conv_s")}
    return tuple(np.ascontiguousarray(v) for v in (
        y[None, :NP], y[None, NP:],
        kv["k"][None, None, :NP], kv["v"][None, None, :NP],
        got["logf_p"].transpose(1, 0, 2).reshape(1, 1, NP, H), conv["conv_p"],
        kv["k"][None, None, NP:], kv["v"][None, None, NP:],
        got["logf_s"][None, None], conv["conv_s"]))
```

```python
from contextlib import ExitStack

import concourse.bass as bass
from concourse import mybir

F32 = mybir.dt.float32
F32R = mybir.dt.float32r
ACT = mybir.ActivationFunctionType
ALU = mybir.AluOpType
AX = mybir.AxisListType

P = 128
D = 2048
KT = D // P
NP = 512
NS = 64
T = NP + NS
HC = T // 2
H = 8
PAST = 1024
CT = PAST // P
QB = NP // P
W = 31
PADW = W - 1
EXT = 2 * PADW + T
ACCW = EXT - PADW
S_ST = PADW + NP
S_U = S_ST + PADW
EPS = 1e-6
SCALE = float(P) ** -0.5
MASKED = -1e30
G_PAST = NP
G_NEW = NP + PAST
GW = NP + PAST + NS

UK = 8
UW = UK * P
RING = 4
LEAD = 3
AHEAD = 7
AK = 4
AW = 2 * P
A_TILES = 8
A_STEPS = 2 * A_TILES
B_TURNS = (2 * KT - H) // 2
N_ADA = RING * KT
N_A = H * A_STEPS
N_B = 4 * B_TURNS
N_C = 2 * KT
D_STEPS = 8
N_D = D_STEPS * KT // 2
A0 = N_ADA
B0 = A0 + N_A
C0 = B0 + N_B
D0 = C0 + N_C
N_UNITS = D0 + N_D
X, Y, Z, V = 4, 5, 6, 7


def build(nc, a, o):
    ctx = ExitStack()
    with ctx:
        top = [((nc.sbuf_base + 63) // 64) * 64]

        def room(nbytes):
            at = top[0]
            top[0] += (nbytes + 31) // 32 * 32
            return at

        def place(name, shape, at, dt=F32):
            return nc.alloc_sbuf_tensor_at(name, shape, dt, offset=at)

        def sb(name, shape, dt=F32):
            n = 4
            for s in shape[1:]:
                n *= s
            return place(name, shape, room(n), dt)

        TB = T * 4
        w_raw = sb("w_raw", [P, RING, UW])
        w_hi = sb("w_hi", [P, RING, UW], F32R)
        w_lo = sb("w_lo", [P, RING, UW], F32R)
        ones = sb("ones", [P, P])
        ident = sb("ident", [P, P])
        upto = sb("upto", [P, P])
        after = sb("after", [P, P])
        causal = sb("causal", [P, P])
        eps_c = sb("eps_c", [P, 1])
        c_in = sb("c_in", [P, KT, 2])
        c_silu = sb("c_silu", [P, KT, 2])
        c_parts = sb("c_parts", [P, 4 * KT + P], F32R)
        pick = sb("pick", [4, 2])
        ada_rows = sb("ada_rows", [4, AW])
        b_ada = sb("b_ada", [P, 3 * KT])
        norm_g = sb("norm_g", [P, KT])
        mod = sb("mod", [P, 2 * KT, 2])
        gate = sb("gate", [P, KT, 2])
        qk_g = sb("qk_g", [P, 2])
        ln_gb = sb("ln_gb", [P, H, 2])
        ln_cur = sb("ln_cur", [P, 2])
        w_f = sb("w_f", [P, KT, H])
        w_f_hi = sb("w_f_hi", [P, KT, H], F32R)
        w_f_lo = sb("w_f_lo", [P, KT, H], F32R)
        b_f = sb("b_f", [P, 5, H])
        z_f = sb("z_f", [P, 5, H])
        e_f = sb("e_f", [P, 5, H])
        logf = sb("logf", [P, 5, H])
        logf_past = sb("logf_past", [P, CT, H])
        conv_w = sb("conv_w", [P, W + 1])
        stat_max = sb("stat_max", [P, 5])
        stat_neg = sb("stat_neg", [P, 5])
        stat_sum = sb("stat_sum", [P, 5])
        stat_inv = sb("stat_inv", [P, 5])
        ch_sum = sb("ch_sum", [P, T])

        h_hi_at = room(KT * TB)
        h_lo_at = room(KT * TB)
        x_at = room((2 * H + 1) * TB)
        s_at = top[0]
        h_hi = place("h_hi", [P, KT, T], h_hi_at, F32R)
        h_lo = place("h_lo", [P, KT, T], h_lo_at, F32R)
        x_t = place("x_t", [P, KT, T], x_at)
        y_a = place("y_a", [P, H, T], x_at)
        cv = place("cv", [P, H + 1, T], x_at + H * TB)
        yb_hi = place("yb_hi", [P, H, T], h_hi_at, F32R)
        yb_lo = place("yb_lo", [P, H, T], h_hi_at + H * TB, F32R)
        mg_hi = place("mg_hi", [P, KT, T], h_lo_at, F32R)
        mg_lo = place("mg_lo", [P, KT, T], x_at, F32R)

        sq_x = place("sq_x", [P, 4, T], s_at)
        rstd_x = place("rstd_x", [P, T], s_at + 4 * TB)
        g_rows = place("g_rows", [H, GW], s_at + 5 * TB)
        g_b = sb("g_b", [P, GW])
        qn = sb("qn", [P, T])
        kn = sb("kn", [P, T])
        vf = sb("vf", [P, T])
        sq = sb("sq", [P, T])
        rs = sb("rs", [P, T])
        v_tok = sb("v_tok", [P, QB + 1, P])
        past = sb("past", [P, PAST])
        s_p = sb("s_p", [P, 2, NP])
        s_s = sb("s_s", [P, PAST + NS])
        p_t = sb("p_t", [P, QB, P])
        ps_t = sb("ps_t", [P, CT, NS])
        pn_t = sb("pn_t", [NS, NS])
        s_gb = sb("s_gb", [P, T])
        sig = sb("sig", [P, T])
        ext = sb("ext", [P, EXT])
        acc = sb("acc", [P, ACCW])
        s_m_at = top[0]
        s_m = sb("s_m", [P, T])
        end_a = top[0]
        top[0] = s_at
        ya_hi = sb("ya_hi", [P, H, T], F32R)
        ya_lo = sb("ya_lo", [P, H, T], F32R)
        b_at = top[0]
        assert b_at + 4 * TB <= s_m_at
        mu = place("mu", [P, T], b_at)
        rstd = place("rstd", [P, T], b_at + TB)
        sq_b = place("sq_b", [P, T], b_at + 2 * TB)
        sq_sum = place("sq_sum", [P, T], b_at + 3 * TB)
        gb_at = end_a
        gb_in = place("gb_in", [P, 2, T], gb_at)
        m_in = place("m_in", [P, 2, 2, T], b_at)
        merge_at = b_at + 4 * TB
        merge = place("merge", [P, T], merge_at)
        merge_b = place("merge_b", [P, T], x_at + 2 * H * TB)
        x_in = place("x_in", [P, 2, T], b_at)
        y_out = place("y_out", [P, 2, T], b_at + 2 * TB)

        ps = ctx.enter_context(nc.psum_tensor("ps", [P, 8, 512], F32))
        g_dram = nc.dram_tensor("g_scratch", [H, GW], F32, kind="Internal").ap()
        gb_dram = nc.dram_tensor("silu_gb_scratch", [H, P, T], F32, kind="Internal").ap()
        m_dram = nc.dram_tensor("sigmoid_m_scratch", [2 * KT, P, T], F32, kind="Internal").ap()

        def sem(name):
            return ctx.enter_context(nc.semaphore(name))

        const_in = sem("const_in")
        x_landed = [sem(f"x_landed{g}") for g in range(4)]
        masks_ready = sem("masks_ready")
        pool_step = sem("pool_step")
        zeroed = sem("zeroed")
        w_landed = [sem(f"w_landed{r}") for r in range(RING)]
        hi_ready, lo_ready, w_used = sem("hi_ready"), sem("lo_ready"), sem("w_used")
        tile_evac = sem("tile_evac")
        silu_c = sem("silu_c")
        sqx_ready, sqx_used = sem("sqx_ready"), sem("sqx_used")
        rstdx_ready, rinv_ready = sem("rstdx_ready"), sem("rinv_ready")
        xn_ready = sem("xn_ready")
        mod_ready = sem("mod_ready")
        parts_ready, pick_ready = sem("parts_ready"), sem("pick_ready")
        rows_ready, cols_done = sem("rows_ready"), sem("cols_done")
        h_ready, h_hi_ready, h_lo_ready = sem("h_ready"), sem("h_hi_ready"), sem("h_lo_ready")
        wf_hi_ready, wf_lo_ready = sem("wf_hi_ready"), sem("wf_lo_ready")
        f_done, f_act, logf_ready, logf_stored = sem("f_done"), sem("f_act"), sem("logf_ready"), sem("logf_stored")
        g_done, g_rows_ready, g_stored, g_landed = sem("g_done"), sem("g_rows_ready"), sem("g_stored"), sem("g_landed")
        sq_ready, ss_done, std_ready = sem("sq_ready"), sem("ss_done"), sem("std_ready")
        qkn_ready, k_stored, v_stored = sem("qkn_ready"), sem("k_stored"), sem("v_stored")
        vt_done, vtok_ready = sem("vt_done"), sem("vtok_ready")
        past_landed = sem("past_landed")
        sc_done, sc_evac, prep_done, exp_done, p_ready = (sem(n) for n in ("sc_done", "sc_evac", "prep_done", "exp_done", "p_ready"))
        tr_done, pt_ready, pv_done, pv_evac = (sem(n) for n in ("tr_done", "pt_ready", "pv_done", "pv_evac"))
        u_ready, conv_done, cw_landed, c_stored = (sem(n) for n in ("u_ready", "conv_done", "cw_landed", "c_stored"))
        gb_stored, m_stored = sem("gb_stored"), sem("m_stored")
        summed = sem("summed")
        mean_done, mu_ready = sem("mean_done"), sem("mu_ready")
        centred, sqb_ready, sq_summed = sem("centred"), sem("sqb_ready"), sem("sq_summed")
        var_done, rstd_ready = sem("var_done"), sem("rstd_ready")
        lncur_ready, scaled, ln_silu = sem("lncur_ready"), sem("scaled"), sem("ln_silu")
        gb_landed = [sem(f"gb_landed{r}") for r in range(2)]
        yb_ready, ya_hi_ready, ya_lo_ready = sem("yb_ready"), sem("ya_hi_ready"), sem("ya_lo_ready")
        yb_hi_ready, yb_lo_ready = sem("yb_hi_ready"), sem("yb_lo_ready")
        m_landed = [sem(f"m_landed{r}") for r in range(2)]
        gate_ready = sem("gate_ready")
        merged, mg_hi_ready, mg_lo_ready = sem("merged"), sem("mg_hi_ready"), sem("mg_lo_ready")
        c_evac = sem("c_evac")
        xin_landed = [sem(f"xin_landed{r}") for r in range(2)]
        y_ready, y_stored = sem("y_ready"), [sem(f"y_stored{r}") for r in range(2)]
        inv_done = sem("inv_done")
        chain = sem("dve_step")

        def banks(b):
            return ps[:, b:b + 2, 0:HC]

        def halves(ap):
            return ap.rearrange("p (c n) -> p c n", c=2)

        def uses(q):
            return 16 * (q + 1)

        block = ctx.enter_context(nc.Block())

        @block.sync
        def _(sp):
            for dst, src in ((c_in, a["c"]), (b_ada, a["b_ada"]), (norm_g, a["norm_g"]), (qk_g, a["qk_g"]),
                             (ln_gb, a["ln_gb"]), (w_f, a["w_f"]), (b_f, a["b_f"]), (logf_past, a["logf_past"])):
                sp.dma_start(dst[:], src).then_inc(const_in, 16)
            def load_unit(n, slot):
                sp.dma_start(w_raw[:, slot], a["w"][n]).then_inc(w_landed[slot], 16)

            for g in range(4):
                sp.dma_start(x_t[:, 4 * g:4 * g + 4], a["x"][:, 4 * g:4 * g + 4]).then_inc(x_landed[g], 16)
            for n in range(RING):
                load_unit(n, n)
            for n in range(RING, AHEAD):
                sp.wait_ge(lo_ready, n - RING + 1)
                load_unit(n, n % RING)
            with sp.Fori(0, KT) as g:
                for u in range(4):
                    sp.wait_ge(lo_ready, 4 * g + u + AHEAD - RING + 1)
                    load_unit(4 * g + u + AHEAD, (u + AHEAD) % RING)
            sp.wait_ge(logf_ready, 1)
            sp.dma_start(o["logf_p"], logf[:, 0:QB]).then_inc(logf_stored, 16)
            sp.dma_start(o["logf_s"], logf[NS:P, QB]).then_inc(logf_stored, 16)
            sp.wait_ge(g_rows_ready, 4)
            sp.dma_start(g_dram, g_rows[:]).then_inc(g_stored, 16)
            sp.wait_ge(g_stored, 16)

            with sp.Fori(0, H) as i:
                for u in range(A_STEPS):
                    sp.wait_ge(lo_ready, A0 + A_STEPS * i + u + AHEAD - RING + 1)
                    load_unit(A0 + A_STEPS * i + u + AHEAD, (u + AHEAD) % RING)
                    if u == 0:
                        sp.wait_ge(pv_done, 5 * i)
                        sp.dma_start(past[:], a["k_past"][i]).then_inc(past_landed, 16)
                        sp.wait_ge(sc_evac, 7 * i)
                        sp.dma_start(g_b[:], g_dram[bass.ds(i, 1), :].to_broadcast([P, GW])).then_inc(g_landed, 16)
                    if u == 6:
                        sp.wait_ge(qkn_ready, 2 * i + 2)
                        sp.dma_start(o["k"][i], kn[:]).then_inc(k_stored, 16)
                    if u == 7:
                        sp.wait_ge(tile_evac, 8 * i + 4)
                        sp.dma_start(o["v"][i], vf[:]).then_inc(v_stored, 16)
                    if u == 11:
                        sp.wait_ge(conv_done, 2 * (i + 1))
                        sp.dma_start(conv_w[:], a["conv_w"][i]).then_inc(cw_landed, 16)
                        sp.dma_start(ext[:, S_ST:S_U], a["state"][i]).then_inc(cw_landed, 16)
                    if u == 12:
                        sp.wait_ge(sc_done, 7 * i + 6)
                        sp.dma_start(past[:], a["v_past"][i]).then_inc(past_landed, 16)
                    if u == 14:
                        sp.wait_ge(u_ready, 2 * (i + 1))
                        sp.dma_start(o["conv_p"][i], ext[:, NP:NP + PADW]).then_inc(c_stored, 16)
                        sp.dma_start(o["conv_s"][i], ext[:, EXT - PADW:EXT]).then_inc(c_stored, 16)
                    if u == 15:
                        sp.wait_ge(tile_evac, 8 * i + 8)
                        sp.dma_start(gb_dram[i], s_gb[:]).then_inc(gb_stored, 16)
                sp.wait_ge(tile_evac, 8 * i + 9)
                sp.dma_start(m_dram[i], s_m[:]).then_inc(m_stored, 16)

            sp.wait_ge(gb_stored, 16 * H)

            def b_turn(t):
                for u in range(4):
                    sp.wait_ge(lo_ready, B0 + 4 * t + u + AHEAD - RING + 1)
                    load_unit(B0 + 4 * t + u + AHEAD, (u + AHEAD) % RING)
                    if u % 2:
                        sp.wait_ge(tile_evac, 8 * H + 2 * t + u // 2 + 2)
                        sp.dma_start(m_dram[2 * t + H + u // 2], s_m[:]).then_inc(m_stored, 16)

            with sp.Fori(0, 7) as t:
                b_turn(t)
            with sp.Fori(0, 4) as t:
                for r in range(2):
                    sp.wait_ge(yb_ready, 2 * t)
                    sp.dma_start(gb_in[:, r], gb_dram[2 * t + r]).then_inc(gb_landed[r], 16)
                b_turn(t + 7)
            b_turn(11)

            sp.wait_ge(m_stored, 16 * 2 * KT)
            sp.wait_ge(yb_lo_ready, H)
            with sp.Fori(0, KT // 2) as t:
                for r in range(2):
                    sp.wait_ge(merged, 2 * t)
                    sp.dma_start(m_in[:, r, 0], m_dram[2 * t + r]).then_inc(m_landed[r], 16)
                    sp.dma_start(m_in[:, r, 1], m_dram[2 * t + r + KT]).then_inc(m_landed[r], 16)
                    for u in (2 * r, 2 * r + 1):
                        sp.wait_ge(lo_ready, C0 + 4 * t + u + AHEAD - RING + 1)
                        load_unit(C0 + 4 * t + u + AHEAD, (u + AHEAD) % RING)

            sp.wait_ge(merged, KT)
            def x_ahead(t):
                for r in range(2):
                    sp.wait_ge(y_ready, 6 * t)
                    sp.dma_start(x_in[:, r], a["xt"][2 * t + r]).then_inc(xin_landed[r], 16)

            def store_y(t):
                for r in range(2):
                    sp.wait_ge(y_ready, 6 * t + 3 * r + 3)
                    sp.dma_start(o["y"][2 * t + r], y_out[:, r]).then_inc(y_stored[r], 16)

            with sp.Fori(0, KT // 2 - 1) as t:
                x_ahead(t)
                for u in range(D_STEPS):
                    sp.wait_ge(lo_ready, D0 + D_STEPS * t + u + AHEAD - RING + 1)
                    load_unit(D0 + D_STEPS * t + u + AHEAD, (u + AHEAD) % RING)
                store_y(t)
            sp.wait_ge(lo_ready, N_UNITS - RING)
            load_unit(N_UNITS - 1, (N_UNITS - 1) % RING)
            x_ahead(KT // 2 - 1)
            store_y(KT // 2 - 1)
            for s, n in ((logf_stored, 2), (k_stored, H), (v_stored, H), (c_stored, 2 * H),
                         (y_stored[0], KT // 2), (y_stored[1], KT // 2)):
                sp.wait_ge(s, 16 * n)

        @block.gpsimd
        def _(pool):
            pool.memset(ones[:], 1.0).then_inc(pool_step, 1)
            pool.memset(eps_c[:], EPS).then_inc(pool_step, 1)
            pool.memset(ident[:], 0.0).then_inc(pool_step, 1)
            pool.memset(causal[:], 0.0).then_inc(pool_step, 1)
            pool.memset(ch_sum[:], 0.0).then_inc(pool_step, 1)
            pool.wait_ge(pool_step, 5)
            pool.affine_select(out=ident[:], in_=ident[:], compare_op=ALU.not_equal, fill=1.0, base=0,
                               pattern=[[-1, P]], channel_multiplier=1).then_inc(masks_ready, 1)
            pool.affine_select(out=upto[:], in_=ones[:], compare_op=ALU.is_ge, fill=0.0, base=0,
                               pattern=[[1, P]], channel_multiplier=-1).then_inc(masks_ready, 1)
            pool.affine_select(out=after[:], in_=ones[:], compare_op=ALU.is_gt, fill=0.0, base=0,
                               pattern=[[-1, P]], channel_multiplier=1).then_inc(masks_ready, 1)
            pool.affine_select(out=causal[:], in_=causal[:], compare_op=ALU.is_ge, fill=MASKED, base=0,
                               pattern=[[-1, P]], channel_multiplier=1).then_inc(masks_ready, 1)
            pool.wait_ge(rinv_ready, 1)
            with pool.Fori(0, KT) as i:
                pool.tensor_tensor(x_t[:, i], x_t[:, i], rstd_x[:], ALU.mult).then_inc(xn_ready, 1)
            with pool.Fori(0, H + 1) as i:
                pool.wait_ge(conv_done, 2 * (i + 1))
                pool.wait_ge(summed, i)
                pool.tensor_tensor(ch_sum[:], ch_sum[:], cv[:, i], ALU.add).then_inc(summed, 1)
            pool.wait_ge(centred, 1)
            pool.memset(sq_sum[:], 0.0).then_inc(sq_summed, 1)
            with pool.Fori(0, H) as i:
                pool.wait_ge(sqb_ready, i + 1)
                pool.wait_ge(sq_summed, i + 1)
                pool.tensor_tensor(sq_sum[:], sq_sum[:], sq_b[:], ALU.add).then_inc(sq_summed, 1)

        @block.scalar
        def _(act):
            act.wait_ge(const_in, 16 * 8)
            act.activation(c_silu[:], c_in[:], ACT.Silu).then_inc(silu_c, 1)
            act.wait_ge(zeroed, 1)
            act.wait_ge(silu_c, 1)
            c_hi = c_parts[:, 0:4 * KT].rearrange("p (k r) -> p k r", r=4)[:, :, 0:2]
            act.activation(c_hi, c_silu[:], ACT.Copy).then_inc(silu_c, 1)
            for k in range(KT):
                if k % 4 == 0:
                    act.wait_ge(x_landed[k // 4], 16)
                if k >= 4:
                    act.wait_ge(sqx_used, k - 3)
                act.activation(sq_x[:, k % 4], x_t[:, k], ACT.Square).then_inc(sqx_ready, 1)

            def hi(slot, use, prior=None):
                act.wait_ge(w_landed[slot], use)
                if prior is not None:
                    act.wait_ge(w_used, prior)
                act.activation(w_hi[:, slot], w_raw[:, slot], ACT.Copy).then_inc(hi_ready, 1)

            for n in range(LEAD):
                hi(n, uses(0))
            act.wait_ge(sqx_used, KT)
            act.wait_ge(masks_ready, 1)
            act.activation(halves(rstd_x[:]), banks(X), ACT.Sqrt, scale=1.0 / D, bias=eps_c[:]).then_inc(rstdx_ready, 1)
            with act.Fori(0, KT) as g:
                for u in range(4):
                    hi((u + LEAD) % RING, uses(g + (u + LEAD) // RING), 4 * g + u)
                act.wait_ge(w_used, 4 * g + 4)
                act.activation(ada_rows[:], ps[0:4, 0, 0:AW], ACT.Copy).then_inc(rows_ready, 1)
                act.wait_ge(h_ready, 2 * g + 2)
                act.activation(h_hi[:, g], x_t[:, g], ACT.Copy).then_inc(h_hi_ready, 1)
            act.activation(w_f_hi[:], w_f[:], ACT.Copy).then_inc(wf_hi_ready, 1)

            act.wait_ge(tile_evac, 1)
            act.activation(e_f[:], z_f[:], ACT.Abs).then_inc(f_act, 1)
            act.wait_ge(f_act, 1)
            act.activation(e_f[:], e_f[:], ACT.Exp, scale=-1.0).then_inc(f_act, 1)
            act.wait_ge(f_act, 2)
            act.activation(e_f[:], e_f[:], ACT.Ln, bias=ones[:, 0:1]).then_inc(f_act, 1)

            act.wait_ge(g_stored, 16)
            with act.Fori(0, H) as i:
                def evac(t, dst, func):
                    return act.activation(dst, banks(2 * (t % 2)), func)

                def norm_root(n, bank):
                    act.wait_ge(ss_done, 2 * i + n + 1)
                    act.wait_ge(qkn_ready, 2 * i + n)
                    act.activation(halves(rs[:]), banks(bank), ACT.Sqrt, scale=1.0 / P, bias=eps_c[:]).then_inc(std_ready, 1)

                def exp(j):
                    act.wait_ge(prep_done, 5 * i + j + 1)
                    s = s_p[:, j % 2, 0:P * (j + 1)] if j < QB else s_s[0:NS]
                    m = P if j < QB else NS
                    act.activation(s, s, ACT.Exp, bias=stat_neg[0:m, j:j + 1], accum_out=stat_sum[0:m, j:j + 1]).then_inc(exp_done, 1)

                def probs_t(j):
                    act.wait_ge(tr_done, 5 * i + j + 1)
                    act.activation(p_t[:, 0:j + 1].rearrange("p j q -> p (j q)"), ps[:, Z, 0:P * (j + 1)], ACT.Copy).then_inc(pt_ready, 1)

                for u in range(A_STEPS):
                    hi((u + LEAD) % RING, uses(A0 // 4 + 4 * i + (u + LEAD) // RING), A0 + A_STEPS * i + u)
                    if u == 2:
                        evac(0, halves(qn[:]), ACT.Copy).then_inc(tile_evac, 1)
                        act.wait_ge(tile_evac, 8 * i + 2)
                        act.activation(sq[:], qn[:], ACT.Square).then_inc(sq_ready, 1)
                    if u == 3:
                        norm_root(0, X)
                    if u == 4:
                        act.wait_ge(k_stored, 16 * i)
                        evac(1, halves(kn[:]), ACT.Copy).then_inc(tile_evac, 1)
                        act.wait_ge(tile_evac, 8 * i + 3)
                        act.activation(sq[:], kn[:], ACT.Square).then_inc(sq_ready, 1)
                    if u == 5:
                        norm_root(1, Z)
                    if u == 6:
                        act.wait_ge(v_stored, 16 * i)
                        evac(2, halves(vf[:]), ACT.Copy).then_inc(tile_evac, 1)
                    if u == 7:
                        act.wait_ge(vt_done, i + 1)
                        act.wait_ge(pv_done, 5 * i)
                        act.activation(v_tok[:, 0:QB].rearrange("p j d -> p (j d)"), ps[:, Z, :], ACT.Copy).then_inc(vtok_ready, 1)
                        act.activation(v_tok[0:NS, QB], ps[0:NS, V, 0:P], ACT.Copy).then_inc(vtok_ready, 1)
                        exp(0)
                    if u == 8:
                        evac(3, halves(y_a[:, i]), ACT.Silu).then_inc(tile_evac, 1)
                        exp(1)
                    if u == 9:
                        probs_t(0)
                        exp(2)
                    if u == 10:
                        act.wait_ge(conv_done, 2 * (i + 1))
                        act.wait_ge(c_stored, 32 * i)
                        act.activation(ext[:, PADW:PADW + HC], ps[:, 0, 0:HC], ACT.Copy)
                        act.activation(ext[:, PADW + HC:S_ST], ps[:, 1, 0:NP - HC], ACT.Copy)
                        act.activation(ext[:, S_U:EXT], ps[:, 1, NP - HC:HC], ACT.Copy).then_inc(tile_evac, 1)
                        probs_t(1)
                        exp(3)
                    if u == 11:
                        probs_t(2)
                    if u == 12:
                        evac(5, halves(sig[:]), ACT.Sigmoid).then_inc(tile_evac, 1)
                        probs_t(3)
                    if u == 13:
                        exp(4)
                    if u == 14:
                        act.wait_ge(gb_stored, 16 * i)
                        evac(6, halves(s_gb[:]), ACT.Silu).then_inc(tile_evac, 1)
                    if u == 15:
                        act.wait_ge(tr_done, 5 * i + 5)
                        act.activation(ps_t[:].rearrange("p j q -> p (j q)"), ps[:, Z, :], ACT.Copy).then_inc(pt_ready, 1)
                        act.activation(pn_t[:], ps[0:NS, X, 0:NS], ACT.Copy).then_inc(pt_ready, 1)
                act.wait_ge(w_used, A0 + A_STEPS * i + 16)
                act.wait_ge(m_stored, 16 * i)
                evac(7, halves(s_m[:]), ACT.Sigmoid).then_inc(tile_evac, 1)

            def b_turn(t, work=lambda r: None):
                for r in range(2):
                    for u in (2 * r, 2 * r + 1):
                        hi((u + LEAD) % RING, uses(B0 // 4 + t + (u + LEAD) // RING), B0 + 4 * t + u)
                    work(r)
                    act.wait_ge(w_used, B0 + 4 * t + 2 * r + 2)
                    act.wait_ge(m_stored, 16 * (H + 2 * t + r))
                    act.activation(halves(s_m[:]), banks(2 * r), ACT.Sigmoid).then_inc(tile_evac, 1)

            with act.Fori(0, 2) as t:
                b_turn(t)
            act.wait_ge(pv_evac, 5 * H)
            act.wait_ge(k_stored, 16 * H)
            act.wait_ge(v_stored, 16 * H)
            act.wait_ge(gb_stored, 16 * H)
            act.wait_ge(conv_done, 2 * (H + 1))
            with act.Fori(2, 6) as t:
                def squares(r):
                    c = 2 * (t - 2) + r
                    act.activation(ya_hi[:, c], y_a[:, c], ACT.Copy).then_inc(ya_hi_ready, 1)
                    act.wait_ge(centred, c + 2)
                    act.wait_ge(sq_summed, c + 1)
                    act.activation(sq_b[:], cv[:, c + 1], ACT.Square).then_inc(sqb_ready, 1)
                b_turn(t, squares)
            b_turn(6)
            act.wait_ge(var_done, 1)
            act.activation(halves(rstd[:]), banks(X), ACT.Sqrt, scale=1.0 / (H * P), bias=eps_c[:]).then_inc(rstd_ready, 1)
            with act.Fori(7, 11) as t:
                def silus(r):
                    c = 2 * (t - 7) + r
                    act.wait_ge(scaled, c + 1)
                    act.activation(cv[:, c + 1], cv[:, c + 1], ACT.Silu, scale=ln_cur[:, 0:1], bias=ln_cur[:, 1:2]).then_inc(ln_silu, 1)
                b_turn(t, silus)
            b_turn(11)
            with act.Fori(0, H) as c:
                act.activation(yb_hi[:, c], cv[:, c + 1], ACT.Copy).then_inc(yb_hi_ready, 1)

            with act.Fori(0, KT // 2) as t:
                for r in range(2):
                    for u in (2 * r, 2 * r + 1):
                        hi((u + LEAD) % RING, uses(C0 // 4 + t + (u + LEAD) // RING), C0 + 4 * t + u)
                    act.wait_ge(merged, 2 * t + r + 1)
                    act.activation(mg_hi[:, 2 * t + r], merge[:], ACT.Copy).then_inc(mg_hi_ready, 1)

            def gate_rows(t):
                act.wait_ge(w_used, D0 + D_STEPS * t + 5)
                act.activation(ada_rows[:], ps[0:4, X, 0:AW], ACT.Copy).then_inc(rows_ready, 1)

            with act.Fori(0, KT // 2 - 1) as t:
                for u in range(D_STEPS):
                    hi((u + LEAD) % RING, uses(D0 // 4 + 2 * t + (u + LEAD) // RING), D0 + D_STEPS * t + u)
                    if u == 5:
                        gate_rows(t)
            last = KT // 2 - 1
            for u in range(D_STEPS - LEAD):
                hi((u + LEAD) % RING, uses(D0 // 4 + 2 * last + (u + LEAD) // RING), D0 + D_STEPS * last + u)
            gate_rows(last)

        @block.vector
        def _(dve):
            base, turn, per, k = [0], [None], [0], [0]

            def step(ins):
                ins.then_inc(chain, 1)
                k[0] += 1
                dve.wait_ge(chain, base[0] + k[0] if turn[0] is None else turn[0] * per[0] + base[0] + k[0])

            def enter(i, n):
                base[0], k[0] = base[0] + k[0], 0
                turn[0], per[0] = i, n

            def leave(turns, first=0):
                assert k[0] == per[0], (k[0], per[0])
                base[0], k[0], turn[0] = base[0] + turns * per[0], 0, None

            dve.memset(c_parts[:].bitcast(F32), 0.0).then_inc(zeroed, 1)
            dve.wait_ge(masks_ready, 1)
            dve.tensor_tensor(pick[:], ident[0:4, 0:2], ident[0:4, 2:4], ALU.add).then_inc(pick_ready, 1)
            dve.wait_ge(silu_c, 2)
            c_part = c_parts[:, 0:4 * KT].rearrange("p (k r) -> p k r", r=4)
            dve.tensor_tensor(c_part[:, :, 2:4], c_silu[:], c_part[:, :, 0:2].bitcast(F32), ALU.subtract).then_inc(parts_ready, 1)

            def lo(ready, slot):
                dve.wait_ge(hi_ready, ready)
                dve.tensor_tensor(w_lo[:, slot], w_raw[:, slot], w_hi[:, slot].bitcast(F32), ALU.subtract).then_inc(lo_ready, 1)

            for n in range(LEAD):
                lo(n + 1, n)
            dve.wait_ge(rstdx_ready, 1)
            dve.reciprocal(rstd_x[:], rstd_x[:]).then_inc(rinv_ready, 1)

            with dve.Fori(0, KT) as g:
                enter(g, 1)
                for u in range(4):
                    lo(4 * g + u + LEAD + 1, (u + LEAD) % RING)
                m = 2 * g
                dve.wait_ge(cols_done, g + 1)
                dve.tensor_scalar(mod[:, m], ps[:, Z, 0:2], b_ada[:, bass.ds(m, 1)], None, ALU.add).then_inc(mod_ready, 1)
                step(dve.tensor_scalar(mod[:, m + 1], ps[:, Z, 2:4], b_ada[:, bass.ds(m + 1, 1)], 1.0, ALU.add, ALU.add))
                dve.tensor_scalar(mod[:, m + 1], mod[:, m + 1], norm_g[:, bass.ds(g, 1)], None, ALU.mult).then_inc(mod_ready, 1)
                dve.wait_ge(mod_ready, m + 2)
                dve.wait_ge(xn_ready, g + 1)
                for lo_, hi_, s in ((0, NP, 0), (NP, T, 1)):
                    dve.tensor_scalar(x_t[:, g, lo_:hi_], x_t[:, g, lo_:hi_], mod[:, m + 1, s:s + 1],
                                      mod[:, m, s:s + 1], ALU.mult, ALU.add).then_inc(h_ready, 1)
                dve.wait_ge(h_hi_ready, g + 1)
                dve.tensor_tensor(h_lo[:, g], x_t[:, g], h_hi[:, g].bitcast(F32), ALU.subtract).then_inc(h_lo_ready, 1)
                leave(KT)
            dve.wait_ge(wf_hi_ready, 1)
            dve.tensor_tensor(w_f_lo[:], w_f[:], w_f_hi[:].bitcast(F32), ALU.subtract).then_inc(wf_lo_ready, 1)

            dve.wait_ge(f_done, 1)
            dve.tensor_tensor(z_f[:], ps[:, 0, 0:5 * H].rearrange("p (t h) -> p t h", h=H), b_f[:], ALU.add).then_inc(tile_evac, 1)
            dve.wait_ge(f_act, 3)
            dve.scalar_tensor_tensor(out=logf[:], in0=z_f[:], scalar=0.0, in1=e_f[:], op0=ALU.min, op1=ALU.subtract).then_inc(logf_ready, 1)
            dve.wait_ge(g_done, 1)
            for bank, at, n, sign in ((X, 0, NP, -1.0), (Y, G_PAST, 512, 1.0), (Z, G_PAST + 512, 512, 1.0), (V, G_NEW, NS, -1.0)):
                dve.tensor_scalar(g_rows[:, at:at + n], ps[0:H, bank, 0:n], sign, None, ALU.mult).then_inc(g_rows_ready, 1)
            dve.wait_ge(g_stored, 16)

            def conv_step(taps, out):
                for w in taps:
                    if w == 0:
                        step(dve.tensor_scalar(acc[:], ext[:, 0:ACCW], conv_w[:, 0:1], conv_w[:, W:W + 1], ALU.mult, ALU.add))
                    elif w < W - 1:
                        step(dve.scalar_tensor_tensor(out=acc[:], in0=ext[:, w:w + ACCW], scalar=conv_w[:, w:w + 1],
                                                      in1=acc[:], op0=ALU.mult, op1=ALU.add))
                    else:
                        for a0, n, c0 in ((0, NP, 0), (S_ST, NS, NP)):
                            dve.scalar_tensor_tensor(out=out[:, c0:c0 + n], in0=ext[:, w + a0:w + a0 + n],
                                                     scalar=conv_w[:, w:w + 1], in1=acc[:, a0:a0 + n],
                                                     op0=ALU.mult, op1=ALU.add).then_inc(conv_done, 1)

            CONV = [range(0, 4)] + [range(4 + 3 * j, 7 + 3 * j) for j in range(9)]
            CONV_STEPS = W - 1
            dve.memset(ext[:], 0.0).then_inc(zeroed, 1)
            dve.memset(conv_w[:], 0.0).then_inc(zeroed, 1)
            dve.memset(s_s[NS:P, 0:P], 0.0).then_inc(zeroed, 1)
            dve.wait_ge(zeroed, 4)

            with dve.Fori(0, H) as i:
                enter(i, CONV_STEPS + 2 + 2 * 5)

                def normed(n, dst):
                    dve.wait_ge(std_ready, 2 * i + n + 1)
                    step(dve.reciprocal(rs[:], rs[:]))
                    dve.scalar_tensor_tensor(out=dst[:], in0=dst[:], scalar=qk_g[:, n:n + 1], in1=rs[:],
                                             op0=ALU.mult, op1=ALU.mult).then_inc(qkn_ready, 1)

                def scores_in(n, dst, bank, bias):
                    dve.wait_ge(sc_done, 7 * i + n + 1)
                    m, w = dst.shape[0], dst.shape[1]
                    dve.scalar_tensor_tensor(out=dst, in0=ps[0:m, bank, 0:w], scalar=SCALE, in1=g_b[0:m, bias:bias + w],
                                             op0=ALU.mult, op1=ALU.add).then_inc(sc_evac, 1)

                def prepare(j, n, s, last, m):
                    dve.wait_ge(sc_evac, 7 * i + n + 1)
                    step(dve.tensor_tensor(s[:, last:last + m], s[:, last:last + m], causal[0:m, 0:m], ALU.add))
                    step(dve.tensor_reduce(stat_max[0:m, j:j + 1], s[:, 0:last + m], AX.X, ALU.max))
                    dve.tensor_scalar(stat_neg[0:m, j:j + 1], stat_max[0:m, j:j + 1], -1.0, None, ALU.mult).then_inc(prep_done, 1)

                def normalise(j, s, m):
                    dve.wait_ge(exp_done, 5 * i + j + 1)
                    dve.reciprocal(stat_inv[0:m, j:j + 1], stat_sum[0:m, j:j + 1]).then_inc(inv_done, 1)
                    dve.wait_ge(inv_done, 5 * i + j + 1)
                    dve.tensor_scalar(s, s, stat_inv[0:m, j:j + 1], None, ALU.mult).then_inc(p_ready, 1)

                def attended(j):
                    dve.wait_ge(pv_done, 5 * i + j + 1)
                    n = P if j < QB else NS
                    y = y_a[:, i, P * j:P * j + n]
                    dve.tensor_tensor(y, y, ps[:, V, 0:n], ALU.mult).then_inc(pv_evac, 1)

                for u in range(A_STEPS):
                    lo(A0 + A_STEPS * i + u + LEAD + 1, (u + LEAD) % RING)
                    if u == 0:
                        dve.wait_ge(u_ready, 2 * i)
                        dve.wait_ge(cw_landed, 32 * i)
                    if u == 3:
                        normed(0, qn)
                    if u == 5:
                        normed(1, kn)
                    if u == 7:
                        dve.wait_ge(g_landed, 16 * (i + 1))
                    if 8 <= u < 12:
                        normalise(u - 8, s_p[:, u % 2, 0:P * (u - 7)], P)
                    if 7 <= u < 11:
                        b = u - 7
                        scores_in(b, s_p[:, b % 2, 0:P * (b + 1)], X + b % 2, 0)
                        prepare(b, b, s_p[:, b % 2], P * b, P)
                    if u == 10:
                        dve.wait_ge(tile_evac, 8 * i + 5)
                    if 10 <= u < 14:
                        attended(u - 10)
                    if u == 11:
                        scores_in(4, s_s[0:NS, 0:512], X, G_PAST)
                    if u == 12:
                        scores_in(5, s_s[0:NS, 512:1024], Y, G_PAST + 512)
                        dve.wait_ge(tile_evac, 8 * i + 7)
                        dve.tensor_tensor(ext[:, PADW:S_ST], ext[:, PADW:S_ST], sig[:, 0:NP], ALU.mult).then_inc(u_ready, 1)
                        dve.tensor_tensor(ext[:, S_U:EXT], ext[:, S_U:EXT], sig[:, NP:T], ALU.mult).then_inc(u_ready, 1)
                    if u == 13:
                        scores_in(6, s_s[0:NS, PAST:PAST + NS], X, G_NEW)
                        prepare(4, 6, s_s[0:NS], PAST, NS)
                    if u == 14:
                        normalise(4, s_s[0:NS], NS)
                    if u < 10:
                        conv_step(CONV[u], cv[:, i])
                attended(4)
                leave(H)

            def b_los(t, work=lambda r: None):
                for r in range(2):
                    for u in (2 * r, 2 * r + 1):
                        lo(B0 + 4 * t + u + LEAD + 1, (u + LEAD) % RING)
                    work(r)

            dve.wait_ge(u_ready, 2 * H)
            dve.wait_ge(cw_landed, 32 * H)
            conv_of = [range(0, 8), range(8, 16), range(16, 24), range(24, 31)]
            b_los(0, lambda r: conv_step(conv_of[r], cv[:, H]))
            b_los(1, lambda r: conv_step(conv_of[2 + r], cv[:, H]))
            dve.wait_ge(mean_done, 1)
            dve.wait_ge(k_stored, 16 * H)
            dve.wait_ge(v_stored, 16 * H)
            dve.wait_ge(gb_stored, 16 * H)
            dve.wait_ge(c_stored, 32 * H)
            dve.tensor_scalar(halves(mu[:]), banks(X), 1.0 / (H * P), None, ALU.mult).then_inc(centred, 1)
            dve.wait_ge(centred, 1)
            with dve.Fori(2, 6) as t:
                def centre(r):
                    c = 2 * (t - 2) + r
                    dve.tensor_tensor(cv[:, c + 1], cv[:, c + 1], mu[:], ALU.subtract).then_inc(centred, 1)
                    dve.wait_ge(ya_hi_ready, c + 1)
                    dve.tensor_tensor(ya_lo[:, c], y_a[:, c], ya_hi[:, c].bitcast(F32), ALU.subtract).then_inc(ya_lo_ready, 1)
                b_los(t, centre)
            b_los(6)
            dve.wait_ge(rstd_ready, 1)
            step(dve.reciprocal(rstd[:], rstd[:]))
            with dve.Fori(7, 11) as t:
                def scale_c(r):
                    c = 2 * (t - 7) + r
                    dve.tensor_copy(ln_cur[:], ln_gb[:, c]).then_inc(lncur_ready, 1)
                    dve.wait_ge(lncur_ready, c + 1)
                    dve.tensor_tensor(cv[:, c + 1], cv[:, c + 1], rstd[:], ALU.mult).then_inc(scaled, 1)
                    dve.wait_ge(ln_silu, c + 1)
                    dve.wait_ge(gb_landed[r], 16 * (t - 6))
                    dve.tensor_tensor(cv[:, c + 1], cv[:, c + 1], gb_in[:, r], ALU.mult).then_inc(yb_ready, 1)
                b_los(t, scale_c)
            b_los(11)
            with dve.Fori(0, H) as c:
                dve.wait_ge(yb_hi_ready, c + 1)
                dve.tensor_tensor(yb_lo[:, c], cv[:, c + 1], yb_hi[:, c].bitcast(F32), ALU.subtract).then_inc(yb_lo_ready, 1)

            with dve.Fori(0, KT // 2) as t:
                enter(t, 2)
                for r in range(2):
                    for u in (2 * r, 2 * r + 1):
                        lo(C0 + 4 * t + u + LEAD + 1, (u + LEAD) % RING)
                    j = 2 * t + r
                    bank = 4 * r
                    dve.wait_ge(w_used, C0 + 4 * t + 2 * r + 2)
                    dve.wait_ge(m_landed[r], 32 * (t + 1))
                    dve.wait_ge(mg_lo_ready, j)
                    dve.tensor_tensor(halves(merge[:]), banks(bank), halves(m_in[:, r, 0]), ALU.mult).then_inc(c_evac, 1)
                    step(dve.tensor_tensor(halves(merge_b[:]), banks(bank + 2), halves(m_in[:, r, 1]), ALU.mult))
                    dve.wait_ge(c_evac, j + 1)
                    dve.tensor_tensor(merge[:], merge[:], merge_b[:], ALU.add).then_inc(merged, 1)
                    dve.wait_ge(mg_hi_ready, j + 1)
                    dve.tensor_tensor(mg_lo[:, j], merge[:], mg_hi[:, j].bitcast(F32), ALU.subtract).then_inc(mg_lo_ready, 1)
                leave(KT // 2)

            def out_tile(t, r):
                j = 2 * t + r
                dve.wait_ge(w_used, D0 + D_STEPS * t + 2 * r + 6)
                dve.wait_ge(xin_landed[r], 16 * (t + 1))
                dve.wait_ge(y_stored[r], 16 * t)
                for bank, lo_, hi_, at, s in ((0, 0, HC, 0, 0), (1, 0, NP - HC, HC, 0), (1, NP - HC, HC, NP, 1)):
                    n = hi_ - lo_
                    dve.scalar_tensor_tensor(out=y_out[:, r, at:at + n], in0=ps[:, 2 * r + bank, lo_:hi_],
                                             scalar=gate[:, j, s:s + 1], in1=x_in[:, r, at:at + n],
                                             op0=ALU.mult, op1=ALU.add).then_inc(y_ready, 1)

            def gate_cols(t):
                dve.wait_ge(cols_done, KT + t + 1)
                for r in range(2):
                    j = 2 * t + r
                    dve.tensor_scalar(gate[:, j], ps[:, Z, 2 * r:2 * r + 2], b_ada[:, bass.ds(j + 2 * KT, 1)], None,
                                      ALU.add).then_inc(gate_ready, 1)
                dve.wait_ge(gate_ready, 2 * t + 2)

            with dve.Fori(0, KT // 2 - 1) as t:
                for u in range(D_STEPS):
                    lo(D0 + D_STEPS * t + u + LEAD + 1, (u + LEAD) % RING)
                    if u == 6:
                        gate_cols(t)
                        out_tile(t, 0)
                out_tile(t, 1)
            for u in range(D_STEPS - LEAD):
                lo(D0 + D_STEPS * (KT // 2 - 1) + u + LEAD + 1, (u + LEAD) % RING)
            gate_cols(KT // 2 - 1)
            for r in range(2):
                out_tile(KT // 2 - 1, r)

        @block.tensor
        def _(pe):
            pe.wait_ge(masks_ready, 4)
            for k in range(KT):
                pe.wait_ge(sqx_ready, k + 1)
                for c in range(2):
                    mm = pe.matmul(ps[:, X + c, 0:HC], ones[:], sq_x[:, k % 4, c * HC:(c + 1) * HC], start=(k == 0), stop=(k == KT - 1))
                mm.then_inc(sqx_used, 1)
            def columns(slot, ready, k0, bank, start, stop):
                pe.wait_ge(hi_ready, ready)
                pe.wait_ge(lo_ready, ready)
                for kk in range(AK):
                    cs = c_parts[:, 4 * (k0 + kk):4 * (k0 + kk) + P]
                    for n, w in enumerate((w_hi, w_lo)):
                        mm = pe.matmul(ps[:, bank, 0:AW], cs, w[:, slot, AW * kk:AW * (kk + 1)],
                                       start=(start and kk == 0 and n == 0), stop=(stop and kk == AK - 1 and n == 1))
                mm.then_inc(w_used, 1)

            def to_columns(group):
                pe.wait_ge(rows_ready, group + 1)
                for m in range(2):
                    mm = pe.matmul(ps[:, Z, 2 * m:2 * m + 2], ada_rows[:, P * m:P * (m + 1)], pick[:], start=True, stop=True)
                mm.then_inc(cols_done, 1)

            pe.wait_ge(parts_ready, 1)
            pe.wait_ge(pick_ready, 1)
            with pe.Fori(0, KT) as g:
                for u in range(4):
                    columns(u, 4 * g + u + 1, AK * u, 0, u == 0, u == 3)
                pe.wait_ge(mod_ready, 2 * g)
                to_columns(g)

            def three(out, w, kk, parts, start, stop):
                (whi, wlo), (xhi, xlo) = w, parts
                n = 0
                for wp, xp in ((whi, xhi), (whi, xlo), (wlo, xhi)):
                    for c in range(2):
                        mm = pe.matmul(out[:, c], wp[:, kk * P:(kk + 1) * P], xp[:, c * HC:(c + 1) * HC],
                                       start=(start and n == 0), stop=(stop and n == 2))
                    n += 1
                return mm

            def unit(ready, slot, bank, src, k0, start, stop):
                pe.wait_ge(hi_ready, ready)
                pe.wait_ge(lo_ready, ready)
                for kk in range(UK):
                    mm = three(banks(bank), (w_hi[:, slot], w_lo[:, slot]), kk, (src[0][:, k0 + kk], src[1][:, k0 + kk]),
                               start and kk == 0, stop and kk == UK - 1)
                mm.then_inc(w_used, 1)

            pe.wait_ge(h_lo_ready, KT)
            pe.wait_ge(wf_lo_ready, 1)
            pe.wait_ge(mod_ready, 2 * KT)
            for tt in range(5):
                at = P * tt if tt < QB else T - P
                for k in range(KT):
                    for n, (x_, w_) in enumerate(((h_hi, w_f_hi), (h_lo, w_f_hi), (h_hi, w_f_lo))):
                        mm = pe.matmul(ps[:, 0, H * tt:H * (tt + 1)], x_[:, k, at:at + P], w_[:, k],
                                       start=(k == 0 and n == 0), stop=(k == KT - 1 and n == 2))
            mm.then_inc(f_done, 1)
            pe.wait_ge(logf_ready, 1)
            for tt in range(QB):
                for t2 in range(tt + 1):
                    pe.matmul(ps[0:H, X, P * tt:P * (tt + 1)], logf[:, t2], ones[:] if t2 < tt else upto[:], start=(t2 == 0), stop=(t2 == tt))
            for tt in range(CT):
                for t2 in range(tt, CT):
                    pe.matmul(ps[0:H, Y + tt // 4, P * (tt % 4):P * (tt % 4 + 1)], logf_past[:, t2], ones[:] if t2 > tt else after[:],
                              start=(t2 == tt), stop=(t2 == CT - 1))
            pe.matmul(ps[0:H, V, 0:NS], logf[NS:P, QB], upto[NS:P, NS:P], start=True, stop=True).then_inc(g_done, 1)
            pe.wait_ge(g_rows_ready, 4)

            h_parts = (h_hi, h_lo)
            with pe.Fori(0, H) as i:
                def square_sum(n, bank):
                    pe.wait_ge(sq_ready, 2 * i + n + 1)
                    for c in range(2):
                        mm = pe.matmul(ps[:, bank + c, 0:HC], ones[:], sq[:, c * HC:(c + 1) * HC], start=True, stop=True)
                    mm.then_inc(ss_done, 1)

                def scores(n, bank, q, keys, evacuated):
                    pe.wait_ge(sc_evac, 7 * i + evacuated)
                    pe.matmul(ps[0:q.shape[1], bank, 0:keys.shape[1]], q, keys, start=True, stop=True).then_inc(sc_done, 1)

                def prompt_scores(b):
                    scores(b, X + b % 2, qn[:, P * b:P * (b + 1)], kn[:, 0:P * (b + 1)], max(b - 1, 0))

                def turn_probs(b):
                    pe.wait_ge(p_ready, 5 * i + b + 1)
                    if b:
                        pe.wait_ge(pt_ready, 6 * i + b)
                    for j in range(b + 1):
                        mm = pe.transpose(ps[:, Z, P * j:P * (j + 1)], s_p[:, b % 2, P * j:P * (j + 1)], ident[:])
                    mm.then_inc(tr_done, 1)

                def values(b):
                    pe.wait_ge(pt_ready, 6 * i + b + 1)
                    pe.wait_ge(pv_evac, 5 * i + b)
                    for j in range(b + 1):
                        mm = pe.matmul(ps[:, V, 0:P], v_tok[:, j], p_t[:, j], start=(j == 0), stop=(j == b))
                    mm.then_inc(pv_done, 1)

                for u in range(A_STEPS):
                    t, half = divmod(u, 2)
                    if half == 0:
                        pe.wait_ge(tile_evac, 8 * i + t)
                    unit(A0 + A_STEPS * i + u + 1, u % RING, 2 * (t % 2), h_parts, UK * half, half == 0, half == 1)
                    if u == 2:
                        pe.wait_ge(pv_evac, 5 * i)
                        square_sum(0, X)
                    if u == 4:
                        square_sum(1, Z)
                    if u == 6:
                        pe.wait_ge(tile_evac, 8 * i + 4)
                        pe.wait_ge(std_ready, 2 * i + 2)
                        for j in range(QB):
                            pe.transpose(ps[:, Z, P * j:P * (j + 1)], vf[:, P * j:P * (j + 1)], ident[:])
                        pe.transpose(ps[0:NS, V, 0:P], vf[:, NP:T], ident[:]).then_inc(vt_done, 1)
                        pe.wait_ge(qkn_ready, 2 * i + 2)
                        prompt_scores(0)
                    if u == 7:
                        prompt_scores(1)
                    if u == 8:
                        pe.wait_ge(vtok_ready, 2 * i + 2)
                        turn_probs(0)
                        prompt_scores(2)
                    if 9 <= u < 13:
                        values(u - 9)
                        if u < 12:
                            turn_probs(u - 8)
                    if u == 9:
                        prompt_scores(3)
                    if u == 10:
                        pe.wait_ge(past_landed, 32 * i + 16)
                        scores(4, X, qn[:, NP:T], past[:, 0:512], 3)
                    if u == 11:
                        scores(5, Y, qn[:, NP:T], past[:, 512:1024], 4)
                    if u == 12:
                        scores(6, X, qn[:, NP:T], kn[:, NP:T], 5)
                    if u == 14:
                        pe.wait_ge(p_ready, 5 * i + 5)
                        pe.wait_ge(pt_ready, 6 * i + 4)
                        pe.transpose(ps[:, Z, 0:P], s_s[:, 0:P], ident[:])
                        for j in range(1, CT):
                            pe.transpose(ps[:, Z, NS * j:NS * (j + 1)], s_s[0:NS, P * j:P * (j + 1)], ident[0:NS, 0:NS])
                        pe.transpose(ps[0:NS, X, 0:NS], s_s[0:NS, PAST:PAST + NS], ident[0:NS, 0:NS]).then_inc(tr_done, 1)
                    if u == 15:
                        pe.wait_ge(pt_ready, 6 * i + 6)
                        pe.wait_ge(pv_evac, 5 * i + 4)
                        pe.wait_ge(past_landed, 32 * i + 32)
                        for j in range(CT):
                            pe.matmul(ps[:, V, 0:NS], past[:, P * j:P * (j + 1)], ps_t[:, j], start=(j == 0), stop=False)
                        pe.matmul(ps[:, V, 0:NS], v_tok[0:NS, QB], pn_t[:], start=False, stop=True).then_inc(pv_done, 1)

            def b_turn(t):
                for u in range(4):
                    if u % 2 == 0:
                        pe.wait_ge(tile_evac, 8 * H + 2 * t + u // 2)
                    unit(B0 + 4 * t + u + 1, u, 2 * (u // 2), h_parts, UK * (u % 2), u % 2 == 0, u % 2 == 1)

            def column_sum(src, done):
                for c in range(2):
                    mm = pe.matmul(ps[:, X + c, 0:HC], ones[:], src[:, c * HC:(c + 1) * HC], start=True, stop=True)
                mm.then_inc(done, 1)

            with pe.Fori(0, 2) as t:
                b_turn(t)
            pe.wait_ge(summed, H + 1)
            column_sum(ch_sum, mean_done)
            with pe.Fori(2, 7) as t:
                b_turn(t)
            pe.wait_ge(sq_summed, H + 1)
            column_sum(sq_sum, var_done)
            with pe.Fori(7, B_TURNS) as t:
                b_turn(t)

            pe.wait_ge(tile_evac, 8 * H + 2 * B_TURNS + 1)
            pe.wait_ge(ya_lo_ready, H)
            pe.wait_ge(rstd_ready, 1)
            def merge_turn(t, first=False):
                for r in range(2):
                    if not first:
                        pe.wait_ge(merged, 2 * t + r - 1)
                    unit(C0 + 4 * t + 2 * r + 1, 2 * r, 4 * r, (ya_hi, ya_lo), 0, True, True)
                    if first:
                        pe.wait_ge(yb_lo_ready, H)
                    unit(C0 + 4 * t + 2 * r + 2, 2 * r + 1, 4 * r + 2, (yb_hi, yb_lo), 0, True, True)

            merge_turn(0, first=True)
            with pe.Fori(1, KT // 2) as t:
                merge_turn(t)

            def out_turn(t, first=False):
                def part(u, r, half):
                    if half == 0 and not first:
                        pe.wait_ge(y_ready, 6 * t + 3 * r - 3)
                    unit(D0 + D_STEPS * t + u + 1, u % RING, 2 * r, (mg_hi, mg_lo), UK * half, half == 0, half == 1)

                def gate_part(u, k):
                    columns(u % RING, D0 + D_STEPS * t + u + 1, AK * k, X, k == 0, k == 3)

                gate_part(0, 0)
                gate_part(1, 1)
                part(2, 0, 0)
                gate_part(3, 2)
                gate_part(4, 3)
                part(5, 0, 1)
                to_columns(KT + t)
                part(6, 1, 0)
                part(7, 1, 1)

            pe.wait_ge(mg_lo_ready, KT)
            out_turn(0, first=True)
            with pe.Fori(1, KT // 2) as t:
                out_turn(t)


def kernel(**inp):
    import numpy as np
    import concourse.bacc as bacc
    from concourse.bass_utils import run_bass_kernel_spmd

    def cols(v):
        return v.reshape(-1, P).T

    def units(w):
        kk, nn = w.shape
        return w.reshape(kk // (P * UK), UK, P, nn // P, P).transpose(3, 0, 2, 1, 4).reshape(-1, P, UW)

    x = np.concatenate([inp["x_prompt"][0], inp["x_sample"][0]], 0)
    xt = x.T.reshape(KT, P, T)
    c = np.concatenate([inp["c_prompt"], inp["c_sample"]], 0)
    n_mod = 2 * KT
    order = [t for k in range(KT) for t in (k, KT + k)]
    ada = inp["w_ada"][0].reshape(KT // AK, AK, P, 3 * KT, P)[:, :, :, order + list(range(n_mod, 3 * KT))]
    ada = ada.reshape(KT // AK, AK, P, 3 * KT // 2, AW).transpose(3, 0, 2, 1, 4).reshape(3 * KT // 2, KT // AK, P, UW)
    b_cols = cols(inp["b_ada"][0])

    w_in = inp["w_in"][0]
    DA = H * P
    parts, at = {}, 0
    for name, n in (("q", DA), ("k", DA), ("v", DA), ("f", H), ("ga", DA), ("gl", DA), ("gg", DA), ("gb", DA), ("ma", D), ("mb", D)):
        parts[name] = w_in[:, at:at + n]
        at += n
    u = {n: units(p).reshape(-1, 2, P, UW) for n, p in parts.items() if n != "f"}
    turns = np.stack([u[n][:H] for n in ("q", "k", "v", "ga", "gl", "gg", "gb", "ma")], 1).reshape(-1, P, UW)
    rest = np.concatenate([u["ma"][H:], u["mb"]], 0).reshape(-1, P, UW)
    w_o = np.stack([units(inp["w_oa"][0]), units(inp["w_ob"][0])], 1).reshape(-1, P, UW)
    w_out = units(inp["w_out"][0]).reshape(KT // 2, 4, P, UW)
    gate = ada[KT:]
    last = np.stack([gate[:, 0], gate[:, 1], w_out[:, 0], gate[:, 2], gate[:, 3], w_out[:, 1], w_out[:, 2], w_out[:, 3]], 1)
    stream = np.concatenate([ada[:KT].reshape(-1, P, UW), turns, rest, w_o, last.reshape(-1, P, UW)], 0)

    arrays = {
        "x": xt.transpose(1, 0, 2),
        "xt": xt,
        "c": c.T.reshape(KT, P, 2).transpose(1, 0, 2),
        "b_ada": np.concatenate([b_cols[:, order], b_cols[:, n_mod:]], 1),
        "norm_g": cols(inp["norm_g"][0]),
        "qk_g": np.stack([inp["q_norm_g"][0], inp["k_norm_g"][0]], 1),
        "ln_gb": np.stack([cols(inp["conv_ln_g"][0]), cols(inp["conv_ln_b"][0])], 2),
        "w_f": parts["f"].reshape(KT, P, H).transpose(1, 0, 2),
        "b_f": np.broadcast_to(inp["b_f"][0], (P, 5, H)),
        "logf_past": inp["cache_logf"][0, 0].reshape(CT, P, H).transpose(1, 0, 2),
        "w": stream,
        "k_past": inp["cache_k"][0, 0].transpose(1, 2, 0),
        "v_past": inp["cache_v"][0, 0].reshape(CT, P, H, P).transpose(2, 1, 0, 3).reshape(H, P, PAST),
        "conv_w": np.concatenate([inp["conv_w"][0].T, inp["conv_b"][0][:, None]], 1).reshape(H, P, W + 1),
        "state": inp["state_conv"][0, 0].T.reshape(H, P, PADW),
    }
    outs = {"y": (KT, P, T), "k": (H, P, T), "v": (H, P, T), "logf_p": (P, QB, H), "logf_s": (NS, H),
            "conv_p": (H, P, PADW), "conv_s": (H, P, PADW)}
    nc = bacc.Bacc("TRN2", target_bir_lowering=False, num_devices=1, dynamic_dma_scratch_size=1024)
    feed, a, o = {}, {}, {}
    for name, v in arrays.items():
        feed[f"in_{name}"] = np.ascontiguousarray(v)
        a[name] = nc.dram_tensor(f"in_{name}", v.shape, F32, kind="ExternalInput").ap()
    for name, shape in outs.items():
        o[name] = nc.dram_tensor(f"out_{name}", shape, F32, kind="ExternalOutput").ap()
    build(nc, a, o)
    r = run_bass_kernel_spmd(nc, [feed], core_ids=[0]).results[0]
    got = {n: np.asarray(r[f"out_{n}"]) for n in outs}

    y = got["y"].reshape(D, T).T
    kv = {n: got[n].transpose(2, 0, 1) for n in ("k", "v")}
    conv = {n: got[n].reshape(DA, PADW).T[None, None] for n in ("conv_p", "conv_s")}
    return tuple(np.ascontiguousarray(v) for v in (
        y[None, :NP], y[None, NP:],
        kv["k"][None, None, :NP], kv["v"][None, None, :NP],
        got["logf_p"].transpose(1, 0, 2).reshape(1, 1, NP, H), conv["conv_p"],
        kv["k"][None, None, NP:], kv["v"][None, None, NP:],
        got["logf_s"][None, None], conv["conv_s"]))
```

```python
from contextlib import ExitStack

import concourse.bass as bass
from concourse import mybir

F32 = mybir.dt.float32
F32R = mybir.dt.float32r
ACT = mybir.ActivationFunctionType
ALU = mybir.AluOpType
AX = mybir.AxisListType

P = 128
D = 2048
KT = D // P
NP = 512
NS = 64
T = NP + NS
HC = T // 2
H = 8
PAST = 1024
CT = PAST // P
QB = NP // P
W = 31
PADW = W - 1
EXT = 2 * PADW + T
ACCW = EXT - PADW
S_ST = PADW + NP
S_U = S_ST + PADW
EPS = 1e-6
SCALE = float(P) ** -0.5
MASKED = -1e30
G_PAST = NP
G_NEW = NP + PAST
GW = NP + PAST + NS

UK = 8
UW = UK * P
FIRST, FIRST_DMA = 1, 16
RING = 4
LEAD = 3
AHEAD = 7
AK = 4
AW = 2 * P
A_TILES = 8
A_STEPS = 2 * A_TILES
EARLY = 2
EW = EARLY * P + H
N_PRE = 4
M_PRE = EARLY + N_PRE // 2
B_TURNS = (2 * KT - H - M_PRE) // 2
N_ADA = RING * KT
N_A = H * A_STEPS
N_B = 4 * B_TURNS
N_C = 2 * KT
D_STEPS = 4
GATE_STEPS = 2 * KT
N_D = D_STEPS * KT // 2
PRE0 = N_ADA
A0 = PRE0 + N_PRE
B0 = A0 + N_A
C0 = B0 + N_B
D0 = C0 + N_C
N_UNITS = D0 + N_D
CENTRE_TURN = 2
LN_TURN = CENTRE_TURN + H // 2
assert B_TURNS == LN_TURN + H // 2
X, Y, Z, V = 4, 5, 6, 7


def build(nc, a, o):
    ctx = ExitStack()
    with ctx:
        top = [((nc.sbuf_base + 63) // 64) * 64]

        def room(nbytes):
            at = top[0]
            top[0] += (nbytes + 31) // 32 * 32
            return at

        def place(name, shape, at, dt=F32):
            return nc.alloc_sbuf_tensor_at(name, shape, dt, offset=at)

        def sb(name, shape, dt=F32):
            n = 4
            for s in shape[1:]:
                n *= s
            return place(name, shape, room(n), dt)

        TB = T * 4
        w_raw = sb("w_raw", [P, RING, UW])
        w_hi = sb("w_hi", [P, RING, UW], F32R)
        w_lo = sb("w_lo", [P, RING, UW], F32R)
        ones = sb("ones", [P, P])
        ident = sb("ident", [P, P])
        upto = sb("upto", [P, P])
        after = sb("after", [P, P])
        causal = sb("causal", [P, P])
        eps_c = sb("eps_c", [P, 1])
        c_in = sb("c_in", [P, KT, 2])
        c_silu = sb("c_silu", [P, KT, 2])
        c_parts = sb("c_parts", [P, 4 * KT + P], F32R)
        pick = sb("pick", [4, 2])
        ada_rows = sb("ada_rows", [4, AW])
        b_ada = sb("b_ada", [P, 3 * KT])
        norm_g = sb("norm_g", [P, KT])
        mod = sb("mod", [P, 2 * KT, 2])
        gate = sb("gate", [P, KT, 2])
        qk_g = sb("qk_g", [P, 2])
        ln_gb = sb("ln_gb", [P, H, 2])
        ln_cur = sb("ln_cur", [P, 2])
        b_f = sb("b_f", [P, 5, H])
        z_f = sb("z_f", [P, 5, H])
        e_f = sb("e_f", [P, 5, H])
        logf = sb("logf", [P, 5, H])
        logf_past = sb("logf_past", [P, CT, H])
        conv_w = sb("conv_w", [P, W + 1])
        stat_max = sb("stat_max", [P, 5])
        stat_neg = sb("stat_neg", [P, 5])
        stat_sum = sb("stat_sum", [P, 5])
        stat_inv = sb("stat_inv", [P, 5])
        ch_sum = sb("ch_sum", [P, T])

        h_hi_at = room(KT * TB)
        h_lo_at = room(KT * TB)
        x_at = room((2 * H + 1) * TB)
        s_at = top[0]
        h_hi = place("h_hi", [P, KT, T], h_hi_at, F32R)
        h_lo = place("h_lo", [P, KT, T], h_lo_at, F32R)
        x_t = place("x_t", [P, KT, T], x_at)
        y_a = place("y_a", [P, H, T], x_at)
        cv = place("cv", [P, H + 1, T], x_at + H * TB)
        yb_hi = place("yb_hi", [P, H, T], h_hi_at, F32R)
        yb_lo = place("yb_lo", [P, H, T], h_hi_at + H * TB, F32R)
        mg_hi = place("mg_hi", [P, KT, T], h_lo_at, F32R)
        mg_lo = place("mg_lo", [P, KT, T], x_at, F32R)

        sq_x = place("sq_x", [P, 4, T], s_at)
        rstd_x = place("rstd_x", [P, T], s_at + 4 * TB)
        g_rows = place("g_rows", [H, GW], s_at + 5 * TB)
        early_at = s_at + 5 * TB + 4 * GW
        w_early = place("w_early", [P, KT, EW], early_at)
        early_hi = place("early_hi", [P, EW + P - H], early_at + 4 * KT * EW, F32R)
        early_lo = place("early_lo", [P, EW + P - H], early_at + 4 * KT * EW + 4 * (EW + P), F32R)
        other_hi = place("other_hi", [P, EW + P - H], early_at + 4 * KT * EW + 8 * (EW + P), F32R)
        other_lo = place("other_lo", [P, EW + P - H], early_at + 4 * KT * EW + 12 * (EW + P), F32R)
        f_rows = place("f_rows", [H, T], early_at + 4 * KT * EW + 16 * (EW + P))
        sum_x = place("sum_x", [P, T], early_at + 4 * KT * EW + 16 * (EW + P) + TB)
        g_b = sb("g_b", [P, GW])
        qn = sb("qn", [P, T])
        kn = sb("kn", [P, T])
        vf = sb("vf", [P, T])
        sq = sb("sq", [P, T])
        rs = sb("rs", [P, T])
        v_tok = sb("v_tok", [P, QB + 1, P])
        past = sb("past", [P, PAST])
        s_p = sb("s_p", [P, 2, NP])
        s_s = sb("s_s", [P, PAST + NS])
        p_t = sb("p_t", [P, QB, P])
        ps_t = sb("ps_t", [P, CT, NS])
        pn_t = sb("pn_t", [NS, NS])
        s_gb = sb("s_gb", [P, T])
        sig = sb("sig", [P, T])
        ext = sb("ext", [P, EXT])
        acc = sb("acc", [P, ACCW])
        s_m_at = top[0]
        s_m = sb("s_m", [P, T])
        end_a = top[0]
        assert early_at + 4 * KT * EW + 16 * (EW + P) + 2 * TB <= s_m_at
        top[0] = s_at
        ya_hi = sb("ya_hi", [P, H, T], F32R)
        ya_lo = sb("ya_lo", [P, H, T], F32R)
        b_at = top[0]
        assert b_at + 4 * TB <= s_m_at
        mu = place("mu", [P, T], b_at)
        rstd = place("rstd", [P, T], b_at + TB)
        sq_b = place("sq_b", [P, T], b_at + 2 * TB)
        sq_sum = place("sq_sum", [P, T], b_at + 3 * TB)
        gb_at = end_a
        gb_in = place("gb_in", [P, 2, T], gb_at)
        m_in = place("m_in", [P, 2, 2, T], b_at)
        merge_at = b_at + 4 * TB
        merge = place("merge", [P, T], merge_at)
        merge_b = place("merge_b", [P, T], x_at + 2 * H * TB)
        x_in = place("x_in", [P, 2, T], b_at)
        y_out = place("y_out", [P, 2, T], b_at + 2 * TB)
        gate_w = place("gate_w", [P, 4, AK, AW], s_at)
        gate_acc = place("gate_acc", [P, 2, AW], s_at + 4 * 4 * AK * AW)
        gate_diag = place("gate_diag", [P, 4, P], s_at + 4 * 4 * AK * AW + 8 * AW)
        gate_sum = place("gate_sum", [P, 4], s_at + 4 * 4 * AK * AW + 8 * AW + 16 * P)
        assert s_at + 4 * 4 * AK * AW + 8 * AW + 16 * P + 16 <= b_at

        ps = ctx.enter_context(nc.psum_tensor("ps", [P, 8, 512], F32))
        g_dram = nc.dram_tensor("g_scratch", [H, GW], F32, kind="Internal").ap()
        gb_dram = nc.dram_tensor("silu_gb_scratch", [H, P, T], F32, kind="Internal").ap()
        m_dram = nc.dram_tensor("sigmoid_m_scratch", [2 * KT, P, T], F32, kind="Internal").ap()

        def sem(name):
            return ctx.enter_context(nc.semaphore(name))

        const_in = sem("const_in")
        x_landed = [sem(f"x_landed{g}") for g in range(4)]
        masks_ready = sem("masks_ready")
        pool_step = sem("pool_step")
        zeroed = sem("zeroed")
        w_landed = [sem(f"w_landed{r}") for r in range(RING)]
        hi_ready, lo_ready, w_used = sem("hi_ready"), sem("lo_ready"), sem("w_used")
        tile_evac = sem("tile_evac")
        silu_c = sem("silu_c")
        sqx_ready, sqx_used = sem("sqx_ready"), sem("sqx_used")
        rstdx_ready, rinv_ready = sem("rstdx_ready"), sem("rinv_ready")
        xn_ready = sem("xn_ready")
        mod_ready = sem("mod_ready")
        parts_ready = sem("parts_ready")
        rows_ready, cols_done = sem("rows_ready"), sem("cols_done")
        pick_ready = sem("pick_ready")
        h_ready, h_hi_ready, h_lo_ready = sem("h_ready"), sem("h_hi_ready"), sem("h_lo_ready")
        early_landed, early_hi_ready, early_lo_ready, early_used = (sem(n) for n in ("early_landed", "early_hi_ready", "early_lo_ready", "early_used"))
        f_rows_ready, f_turned, pre_evac = sem("f_rows_ready"), sem("f_turned"), sem("pre_evac")
        gp_done = sem("gp_done")
        f_done, f_act, logf_ready, logf_stored = sem("f_done"), sem("f_act"), sem("logf_ready"), sem("logf_stored")
        g_done, g_rows_ready, g_stored, g_landed = sem("g_done"), sem("g_rows_ready"), sem("g_stored"), sem("g_landed")
        sq_ready, ss_done, std_ready = sem("sq_ready"), sem("ss_done"), sem("std_ready")
        qkn_ready, k_stored, v_stored = sem("qkn_ready"), sem("k_stored"), sem("v_stored")
        vt_done, vtok_ready = sem("vt_done"), sem("vtok_ready")
        past_landed = sem("past_landed")
        sc_done, sc_evac, prep_done, exp_done, p_ready = (sem(n) for n in ("sc_done", "sc_evac", "prep_done", "exp_done", "p_ready"))
        tr_done, pt_ready, pv_done, pv_evac = (sem(n) for n in ("tr_done", "pt_ready", "pv_done", "pv_evac"))
        u_ready, conv_done, cw_landed, c_stored = (sem(n) for n in ("u_ready", "conv_done", "cw_landed", "c_stored"))
        gb_stored, m_stored = sem("gb_stored"), sem("m_stored")
        summed = sem("summed")
        mean_done, sumx_done = sem("mean_done"), sem("sumx_done")
        centred, sqb_ready, sq_summed = sem("centred"), sem("sqb_ready"), sem("sq_summed")
        var_done, rstd_ready = sem("var_done"), sem("rstd_ready")
        lncur_ready, scaled, ln_silu = sem("lncur_ready"), sem("scaled"), sem("ln_silu")
        gb_landed = [sem(f"gb_landed{r}") for r in range(2)]
        yb_ready, ya_hi_ready, ya_lo_ready = sem("yb_ready"), sem("ya_hi_ready"), sem("ya_lo_ready")
        yb_hi_ready, yb_lo_ready = sem("yb_hi_ready"), sem("yb_lo_ready")
        m_landed = [sem(f"m_landed{r}") for r in range(2)]
        gate_landed = [sem(f"gate_landed{q}") for q in range(4)]
        gate_step, gate_summed, gate_diag_ready, gate_ready = (
            sem(n) for n in ("gate_step", "gate_summed", "gate_diag_ready", "gate_ready"))
        merged, mg_hi_ready, mg_lo_ready = sem("merged"), sem("mg_hi_ready"), sem("mg_lo_ready")
        c_evac = sem("c_evac")
        xin_landed = [sem(f"xin_landed{r}") for r in range(2)]
        y_ready, y_stored = sem("y_ready"), [sem(f"y_stored{r}") for r in range(2)]
        inv_done = sem("inv_done")
        chain = sem("dve_step")

        def banks(b):
            return ps[:, b:b + 2, 0:HC]

        def halves(ap):
            return ap.rearrange("p (c n) -> p c n", c=2)

        def uses(q):
            return 16 * (q + 1)

        def start(engine, semaphores, first):
            for s in semaphores:
                engine.sem_inc(s, first)

        block = ctx.enter_context(nc.Block())

        @block.sync
        def _(sp):
            start(sp, (k_stored, v_stored, c_stored, gb_stored, cw_landed, *y_stored), FIRST_DMA)
            def load_x(g):
                sp.dma_start(x_t[:, 4 * g:4 * g + 4], a["x"][:, 4 * g:4 * g + 4]).then_inc(x_landed[g], 16)

            load_x(0)
            for dst, src in ((c_in, a["c"]), (b_ada, a["b_ada"]), (norm_g, a["norm_g"]), (qk_g, a["qk_g"]),
                             (ln_gb, a["ln_gb"]), (b_f, a["b_f"]), (logf_past, a["logf_past"])):
                sp.dma_start(dst[:], src).then_inc(const_in, 16)

            def load_unit(n, slot):
                sp.dma_start(w_raw[:, slot], a["w"][n]).then_inc(w_landed[slot], 16)

            for g in range(1, 4):
                load_x(g)
            for n in range(RING):
                load_unit(n, n)
            for n in range(RING, AHEAD):
                sp.wait_ge(lo_ready, n - RING + 1)
                load_unit(n, n % RING)

            def load_early(q):
                sp.dma_start(w_early[:, 4 * q:4 * q + 4], a["w_early"][:, 4 * q:4 * q + 4]).then_inc(early_landed, 16)

            load_early(0)

            def load_ada(g, u):
                sp.wait_ge(lo_ready, 4 * g + u + AHEAD - RING + 1)
                load_unit(4 * g + u + AHEAD, (u + AHEAD) % RING)

            for g in range(2):
                for u in range(4):
                    load_ada(g, u)
                    if (g, u) in ((0, 1), (0, 3), (1, 1)):
                        load_early(1 + 2 * g + u // 2)
            with sp.Fori(2, KT) as g:
                for u in range(4):
                    load_ada(g, u)

            def store_pre(k):
                sp.wait_ge(pre_evac, k + 1)
                sp.dma_start(m_dram[H + (0, 2, 1, 3)[k]], s_m[:]).then_inc(m_stored, 16)

            for u in range(N_PRE):
                sp.wait_ge(lo_ready, PRE0 + u + AHEAD - RING + 1)
                load_unit(PRE0 + u + AHEAD, (u + AHEAD) % RING)
                if u == 1:
                    sp.wait_ge(logf_ready, 1)
                    sp.dma_start(o["logf_p"], logf[:, 0:QB]).then_inc(logf_stored, 16)
                    sp.dma_start(o["logf_s"], logf[NS:P, QB]).then_inc(logf_stored, 16)
                if u >= 1:
                    store_pre(u - 1)
            sp.wait_ge(g_rows_ready, 4)
            sp.dma_start(g_dram, g_rows[:]).then_inc(g_stored, 16)
            sp.wait_ge(g_stored, 16)
            store_pre(M_PRE - 1)

            with sp.Fori(0, H) as i:
                for u in range(A_STEPS):
                    sp.wait_ge(lo_ready, A0 + A_STEPS * i + u + AHEAD - RING + 1)
                    load_unit(A0 + A_STEPS * i + u + AHEAD, (u + AHEAD) % RING)
                    if u == 0:
                        sp.wait_ge(pv_done, FIRST + 5 * i)
                        sp.dma_start(past[:], a["k_past"][i]).then_inc(past_landed, 16)
                        sp.wait_ge(sc_evac, FIRST + 7 * i)
                        sp.dma_start(g_b[:], g_dram[bass.ds(i, 1), :].to_broadcast([P, GW])).then_inc(g_landed, 16)
                    if u == 6:
                        sp.wait_ge(qkn_ready, FIRST + 2 * i + 2)
                        sp.dma_start(o["k"][i], kn[:]).then_inc(k_stored, 16)
                    if u == 7:
                        sp.wait_ge(tile_evac, FIRST + 8 * i + 4)
                        sp.dma_start(o["v"][i], vf[:]).then_inc(v_stored, 16)
                    if u == 11:
                        sp.wait_ge(conv_done, 2 * (i + 1))
                        sp.dma_start(conv_w[:], a["conv_w"][i]).then_inc(cw_landed, 16)
                        sp.dma_start(ext[:, S_ST:S_U], a["state"][i]).then_inc(cw_landed, 16)
                    if u == 12:
                        sp.wait_ge(sc_done, 7 * i + 6)
                        sp.dma_start(past[:], a["v_past"][i]).then_inc(past_landed, 16)
                    if u == 14:
                        sp.wait_ge(u_ready, FIRST + 2 * (i + 1))
                        sp.dma_start(o["conv_p"][i], ext[:, NP:NP + PADW]).then_inc(c_stored, 16)
                        sp.dma_start(o["conv_s"][i], ext[:, EXT - PADW:EXT]).then_inc(c_stored, 16)
                    if u == 15:
                        sp.wait_ge(tile_evac, FIRST + 8 * i + 8)
                        sp.dma_start(gb_dram[i], s_gb[:]).then_inc(gb_stored, 16)
                sp.wait_ge(tile_evac, FIRST + 8 * i + 9)
                sp.dma_start(m_dram[i], s_m[:]).then_inc(m_stored, 16)

            sp.wait_ge(gb_stored, FIRST_DMA + 16 * H)

            def b_turn(t):
                for u in range(4):
                    sp.wait_ge(lo_ready, B0 + 4 * t + u + AHEAD - RING + 1)
                    load_unit(B0 + 4 * t + u + AHEAD, (u + AHEAD) % RING)
                    if u % 2:
                        sp.wait_ge(tile_evac, FIRST + 8 * H + 2 * t + u // 2 + 2)
                        sp.dma_start(m_dram[2 * t + H + M_PRE + u // 2], s_m[:]).then_inc(m_stored, 16)

            with sp.Fori(0, LN_TURN) as t:
                b_turn(t)
            with sp.Fori(0, H // 2) as t:
                for r in range(2):
                    sp.wait_ge(yb_ready, FIRST + 2 * t)
                    sp.dma_start(gb_in[:, r], gb_dram[2 * t + r]).then_inc(gb_landed[r], 16)
                b_turn(t + LN_TURN)

            sp.wait_ge(m_stored, 16 * 2 * KT)
            sp.wait_ge(yb_lo_ready, H)
            with sp.Fori(0, KT // 2) as t:
                for r in range(2):
                    sp.wait_ge(merged, FIRST + 2 * t)
                    sp.dma_start(m_in[:, r, 0], m_dram[2 * t + r]).then_inc(m_landed[r], 16)
                    sp.dma_start(m_in[:, r, 1], m_dram[2 * t + r + KT]).then_inc(m_landed[r], 16)
                    for u in (2 * r, 2 * r + 1):
                        sp.wait_ge(lo_ready, C0 + 4 * t + u + AHEAD - RING + 1)
                        load_unit(C0 + 4 * t + u + AHEAD, (u + AHEAD) % RING)

            sp.wait_ge(w_used, C0 + N_C - 2)
            for q in range(4):
                sp.dma_start(gate_w[:, q], a["w_gate"][q]).then_inc(gate_landed[q], 16)
            sp.wait_ge(merged, FIRST + KT)

            def x_ahead(t):
                for r in range(2):
                    sp.wait_ge(y_ready, FIRST + 6 * t)
                    sp.dma_start(x_in[:, r], a["xt"][2 * t + r]).then_inc(xin_landed[r], 16)

            def store_y(t):
                for r in range(2):
                    sp.wait_ge(y_ready, FIRST + 6 * t + 3 * r + 3)
                    sp.dma_start(o["y"][2 * t + r], y_out[:, r]).then_inc(y_stored[r], 16)

            def load_gate(t, q):
                sp.dma_start(gate_w[:, q], a["w_gate"][4 * t + q]).then_inc(gate_landed[q], 16)

            def gate_ahead(t):
                for q in range(4):
                    sp.wait_ge(gate_step, GATE_STEPS * t + 2 * AK * (q + 1))
                    load_gate(t + 1, q)

            with sp.Fori(0, KT // 2 - 2) as t:
                x_ahead(t)
                for u in range(D_STEPS):
                    sp.wait_ge(lo_ready, D0 + D_STEPS * t + u + AHEAD - RING + 1)
                    load_unit(D0 + D_STEPS * t + u + AHEAD, (u + AHEAD) % RING)
                    if u == 1:
                        gate_ahead(t)
                store_y(t)
            sp.wait_ge(lo_ready, N_UNITS - RING)
            load_unit(N_UNITS - 1, (N_UNITS - 1) % RING)
            x_ahead(KT // 2 - 2)
            gate_ahead(KT // 2 - 2)
            store_y(KT // 2 - 2)
            x_ahead(KT // 2 - 1)
            store_y(KT // 2 - 1)
            sp.wait_ge(logf_stored, 16 * 2)
            for s, n in ((k_stored, H), (v_stored, H), (c_stored, 2 * H), (y_stored[0], KT // 2), (y_stored[1], KT // 2)):
                sp.wait_ge(s, FIRST_DMA + 16 * n)

        @block.gpsimd
        def _(pool):
            start(pool, (summed,), FIRST)
            pool.memset(ones[:], 1.0).then_inc(pool_step, 1)
            pool.memset(eps_c[:], EPS).then_inc(pool_step, 1)
            pool.memset(ident[:], 0.0).then_inc(pool_step, 1)
            pool.memset(causal[:], 0.0).then_inc(pool_step, 1)
            pool.memset(ch_sum[:], 0.0).then_inc(pool_step, 1)
            pool.wait_ge(pool_step, 5)
            pool.affine_select(out=ident[:], in_=ident[:], compare_op=ALU.not_equal, fill=1.0, base=0,
                               pattern=[[-1, P]], channel_multiplier=1).then_inc(masks_ready, 1)
            pool.affine_select(out=upto[:], in_=ones[:], compare_op=ALU.is_ge, fill=0.0, base=0,
                               pattern=[[1, P]], channel_multiplier=-1).then_inc(masks_ready, 1)
            pool.affine_select(out=after[:], in_=ones[:], compare_op=ALU.is_gt, fill=0.0, base=0,
                               pattern=[[-1, P]], channel_multiplier=1).then_inc(masks_ready, 1)
            pool.affine_select(out=causal[:], in_=causal[:], compare_op=ALU.is_ge, fill=MASKED, base=0,
                               pattern=[[-1, P]], channel_multiplier=1).then_inc(masks_ready, 1)
            pool.wait_ge(rinv_ready, 2)
            def normalised(k):
                pool.tensor_tensor(x_t[:, k], x_t[:, k], rstd_x[:], ALU.mult).then_inc(xn_ready, 1)

            def low_parts(k, e_hi=early_hi, e_lo=early_lo):
                pool.wait_ge(h_hi_ready, k + 1)
                pool.tensor_tensor(h_lo[:, k], x_t[:, k], h_hi[:, k].bitcast(F32), ALU.subtract).then_inc(h_lo_ready, 1)
                pool.wait_ge(early_hi_ready, k + 1)
                pool.tensor_tensor(e_lo[:, 0:EW], w_early[:, k], e_hi[:, 0:EW].bitcast(F32), ALU.subtract).then_inc(early_lo_ready, 1)

            for k in range(2):
                normalised(k)
            with pool.Fori(0, KT - 2) as k:
                normalised(k + 2)
                low_parts(k)
            low_parts(KT - 2, other_hi, other_lo)
            low_parts(KT - 1)
            with pool.Fori(0, H + 1) as i:
                pool.wait_ge(conv_done, 2 * (i + 1))
                pool.wait_ge(summed, FIRST + i)
                pool.tensor_tensor(ch_sum[:], ch_sum[:], cv[:, i], ALU.add).then_inc(summed, 1)
            pool.wait_ge(centred, 1)
            pool.memset(sq_sum[:], 0.0).then_inc(sq_summed, 1)
            with pool.Fori(0, H) as i:
                pool.wait_ge(sqb_ready, i + 1)
                pool.wait_ge(sq_summed, i + 1)
                pool.tensor_tensor(sq_sum[:], sq_sum[:], sq_b[:], ALU.add).then_inc(sq_summed, 1)

        @block.scalar
        def _(act):
            start(act, (sc_evac, tile_evac, pv_evac, qkn_ready), FIRST)
            act.wait_ge(const_in, 16 * 7)
            act.activation(c_silu[:], c_in[:], ACT.Silu).then_inc(silu_c, 1)
            act.wait_ge(zeroed, 1)
            act.wait_ge(silu_c, 1)
            c_hi = c_parts[:, 0:4 * KT].rearrange("p (k r) -> p k r", r=4)[:, :, 0:2]
            act.activation(c_hi, c_silu[:], ACT.Copy).then_inc(silu_c, 1)

            def square_of_x(k):
                if k % 4 == 0:
                    act.wait_ge(x_landed[k // 4], 16)
                if k >= 4:
                    act.wait_ge(sqx_used, k - 3)
                act.activation(sq_x[:, k % 4], x_t[:, k], ACT.Square).then_inc(sqx_ready, 1)

            def hi(slot, use, prior=None):
                act.wait_ge(w_landed[slot], use)
                if prior is not None:
                    act.wait_ge(w_used, prior)
                act.activation(w_hi[:, slot], w_raw[:, slot], ACT.Copy).then_inc(hi_ready, 1)

            for k in range(KT):
                square_of_x(k)
                if k >= KT - LEAD:
                    hi(k - (KT - LEAD), uses(0))
            act.wait_ge(sumx_done, 1)
            act.activation(halves(rstd_x[:]), banks(X), ACT.Sqrt, scale=1.0 / D, bias=eps_c[:]).then_inc(rstdx_ready, 1)

            def ada_group(g, first=False, k=None, work=lambda u: None):
                for u in range(4):
                    if u == 3:
                        act.wait_ge(w_used, 4 * g + 4)
                        act.activation(ada_rows[:], ps[0:4, 0, 0:AW], ACT.Copy).then_inc(rows_ready, 1)
                    hi((u + LEAD) % RING, uses(g + (u + LEAD) // RING), 4 * g + u if not (first and u == 0) else None)
                    if k is not None and u == 0:
                        early_high(k - 1)
                    if k is not None and u == 2:
                        h_high(k)
                    work(u)

            def h_high(k):
                act.wait_ge(h_ready, 2 * k + 2)
                act.activation(h_hi[:, k], x_t[:, k], ACT.Copy).then_inc(h_hi_ready, 1)

            def early_high(k, first=False):
                if not first:
                    act.wait_ge(early_used, k)
                act.activation(early_hi[:, 0:EW], w_early[:, k], ACT.Copy).then_inc(early_hi_ready, 1)

            ada_group(0, first=True)
            ada_group(1)
            ada_group(2, work=lambda u: h_high(0) if u == 2 else None)

            def first_parts(u):
                if u == 0:
                    act.wait_ge(early_landed, 16 * 4)
                    act.wait_ge(zeroed, 5)
                    early_high(0, first=True)
                if u == 2:
                    h_high(1)

            ada_group(3, work=first_parts)
            with act.Fori(4, KT) as g:
                ada_group(g, k=g - 2)
            early_high(KT - 3)
            h_high(KT - 2)
            act.activation(other_hi[:, 0:EW], w_early[:, KT - 2], ACT.Copy).then_inc(early_hi_ready, 1)
            h_high(KT - 1)
            act.wait_ge(early_used, KT - 2)
            act.activation(early_hi[:, 0:EW], w_early[:, KT - 1], ACT.Copy).then_inc(early_hi_ready, 1)

            def pre_hi(u):
                hi((u + LEAD) % RING, uses((PRE0 + u + LEAD) // RING), PRE0 + u)

            def pre_out(k, bank):
                if k:
                    act.wait_ge(m_stored, 16 * k)
                act.activation(halves(s_m[:]), banks(bank), ACT.Sigmoid).then_inc(pre_evac, 1)

            act.wait_ge(f_done, 1)
            act.activation(halves(f_rows[:]), ps[0:H, 2:4, 0:HC], ACT.Copy).then_inc(f_rows_ready, 1)
            pre_hi(0)
            act.wait_ge(tile_evac, FIRST + 1)
            act.activation(e_f[:], z_f[:], ACT.Abs).then_inc(f_act, 1)
            act.wait_ge(f_act, 1)
            act.activation(e_f[:], e_f[:], ACT.Exp, scale=-1.0).then_inc(f_act, 1)
            act.wait_ge(f_act, 2)
            act.activation(e_f[:], e_f[:], ACT.Ln, bias=ones[:, 0:1]).then_inc(f_act, 1)
            act.wait_ge(early_used, KT)
            pre_out(0, 4)
            pre_hi(1)
            pre_hi(2)
            pre_out(1, 0)
            pre_out(2, 6)
            pre_hi(3)
            act.wait_ge(w_used, PRE0 + N_PRE)
            pre_out(3, 4)
            act.wait_ge(g_stored, 16)
            with act.Fori(0, H) as i:
                def evac(t, dst, func):
                    return act.activation(dst, banks(2 * (t % 2)), func)

                def norm_root(n, bank):
                    act.wait_ge(ss_done, 2 * i + n + 1)
                    act.wait_ge(qkn_ready, FIRST + 2 * i + n)
                    act.activation(halves(rs[:]), banks(bank), ACT.Sqrt, scale=1.0 / P, bias=eps_c[:]).then_inc(std_ready, 1)

                def exp(j):
                    act.wait_ge(prep_done, 5 * i + j + 1)
                    s = s_p[:, j % 2, 0:P * (j + 1)] if j < QB else s_s[0:NS]
                    m = P if j < QB else NS
                    act.activation(s, s, ACT.Exp, bias=stat_neg[0:m, j:j + 1], accum_out=stat_sum[0:m, j:j + 1]).then_inc(exp_done, 1)

                def probs_t(j):
                    act.wait_ge(tr_done, 5 * i + j + 1)
                    act.activation(p_t[:, 0:j + 1].rearrange("p j q -> p (j q)"), ps[:, Z, 0:P * (j + 1)], ACT.Copy).then_inc(pt_ready, 1)

                for u in range(A_STEPS):
                    hi((u + LEAD) % RING, uses(A0 // 4 + 4 * i + (u + LEAD) // RING), A0 + A_STEPS * i + u)
                    if u == 2:
                        evac(0, halves(qn[:]), ACT.Copy).then_inc(tile_evac, 1)
                        act.wait_ge(tile_evac, FIRST + 8 * i + 2)
                        act.activation(sq[:], qn[:], ACT.Square).then_inc(sq_ready, 1)
                    if u == 3:
                        norm_root(0, X)
                    if u == 4:
                        act.wait_ge(k_stored, FIRST_DMA + 16 * i)
                        evac(1, halves(kn[:]), ACT.Copy).then_inc(tile_evac, 1)
                        act.wait_ge(tile_evac, FIRST + 8 * i + 3)
                        act.activation(sq[:], kn[:], ACT.Square).then_inc(sq_ready, 1)
                    if u == 5:
                        norm_root(1, Z)
                    if u == 6:
                        act.wait_ge(v_stored, FIRST_DMA + 16 * i)
                        evac(2, halves(vf[:]), ACT.Copy).then_inc(tile_evac, 1)
                    if u == 7:
                        act.wait_ge(vt_done, i + 1)
                        act.wait_ge(pv_done, FIRST + 5 * i)
                        act.activation(v_tok[:, 0:QB].rearrange("p j d -> p (j d)"), ps[:, Z, :], ACT.Copy).then_inc(vtok_ready, 1)
                        act.activation(v_tok[0:NS, QB], ps[0:NS, V, 0:P], ACT.Copy).then_inc(vtok_ready, 1)
                        exp(0)
                    if u == 8:
                        evac(3, halves(y_a[:, i]), ACT.Silu).then_inc(tile_evac, 1)
                        exp(1)
                    if u == 9:
                        probs_t(0)
                        exp(2)
                    if u == 10:
                        act.wait_ge(conv_done, 2 * (i + 1))
                        act.wait_ge(c_stored, FIRST_DMA + 32 * i)
                        act.activation(ext[:, PADW:PADW + HC], ps[:, 0, 0:HC], ACT.Copy)
                        act.activation(ext[:, PADW + HC:S_ST], ps[:, 1, 0:NP - HC], ACT.Copy)
                        act.activation(ext[:, S_U:EXT], ps[:, 1, NP - HC:HC], ACT.Copy).then_inc(tile_evac, 1)
                        probs_t(1)
                        exp(3)
                    if u == 11:
                        probs_t(2)
                    if u == 12:
                        evac(5, halves(sig[:]), ACT.Sigmoid).then_inc(tile_evac, 1)
                        probs_t(3)
                    if u == 13:
                        exp(4)
                    if u == 14:
                        act.wait_ge(gb_stored, FIRST_DMA + 16 * i)
                        evac(6, halves(s_gb[:]), ACT.Silu).then_inc(tile_evac, 1)
                    if u == 15:
                        act.wait_ge(tr_done, 5 * i + 5)
                        act.activation(ps_t[:].rearrange("p j q -> p (j q)"), ps[:, Z, :], ACT.Copy).then_inc(pt_ready, 1)
                        act.activation(pn_t[:], ps[0:NS, X, 0:NS], ACT.Copy).then_inc(pt_ready, 1)
                act.wait_ge(w_used, A0 + A_STEPS * i + 16)
                act.wait_ge(m_stored, 16 * (M_PRE + i))
                evac(7, halves(s_m[:]), ACT.Sigmoid).then_inc(tile_evac, 1)

            def b_turn(t, work=lambda r: None):
                for r in range(2):
                    for u in (2 * r, 2 * r + 1):
                        hi((u + LEAD) % RING, uses(B0 // 4 + t + (u + LEAD) // RING), B0 + 4 * t + u)
                    work(r)
                    act.wait_ge(w_used, B0 + 4 * t + 2 * r + 2)
                    act.wait_ge(m_stored, 16 * (H + M_PRE + 2 * t + r))
                    act.activation(halves(s_m[:]), banks(2 * r), ACT.Sigmoid).then_inc(tile_evac, 1)

            with act.Fori(0, CENTRE_TURN) as t:
                b_turn(t)
            act.wait_ge(pv_evac, FIRST + 5 * H)
            act.wait_ge(k_stored, FIRST_DMA + 16 * H)
            act.wait_ge(v_stored, FIRST_DMA + 16 * H)
            act.wait_ge(gb_stored, FIRST_DMA + 16 * H)
            act.wait_ge(conv_done, 2 * (H + 1))
            with act.Fori(CENTRE_TURN, LN_TURN) as t:
                def squares(r):
                    c = 2 * (t - CENTRE_TURN) + r
                    act.activation(ya_hi[:, c], y_a[:, c], ACT.Copy).then_inc(ya_hi_ready, 1)
                    act.wait_ge(centred, c + 2)
                    act.wait_ge(sq_summed, c + 1)
                    act.activation(sq_b[:], cv[:, c + 1], ACT.Square).then_inc(sqb_ready, 1)
                b_turn(t, squares)
            act.wait_ge(var_done, 1)
            act.activation(halves(rstd[:]), banks(X), ACT.Sqrt, scale=1.0 / (H * P), bias=eps_c[:]).then_inc(rstd_ready, 1)
            with act.Fori(LN_TURN, B_TURNS) as t:
                def silus(r):
                    c = 2 * (t - LN_TURN) + r
                    act.wait_ge(scaled, c + 1)
                    act.activation(cv[:, c + 1], cv[:, c + 1], ACT.Silu, scale=ln_cur[:, 0:1], bias=ln_cur[:, 1:2]).then_inc(ln_silu, 1)
                b_turn(t, silus)
            with act.Fori(0, H) as c:
                act.wait_ge(yb_ready, FIRST + c + 1)
                act.activation(yb_hi[:, c], cv[:, c + 1], ACT.Copy).then_inc(yb_hi_ready, 1)

            with act.Fori(0, KT // 2) as t:
                for u in range(4):
                    hi((u + LEAD) % RING, uses(C0 // 4 + t + (u + LEAD) // RING), C0 + 4 * t + u)
                for r in range(2):
                    act.wait_ge(merged, FIRST + 2 * t + r + 1)
                    act.activation(mg_hi[:, 2 * t + r], merge[:], ACT.Copy).then_inc(mg_hi_ready, 1)

            with act.Fori(0, KT // 2 - 1) as t:
                for u in range(D_STEPS):
                    hi((u + LEAD) % RING, uses(D0 // 4 + t + (u + LEAD) // RING), D0 + D_STEPS * t + u)
            last = KT // 2 - 1
            for u in range(D_STEPS - LEAD):
                hi((u + LEAD) % RING, uses(D0 // 4 + last + (u + LEAD) // RING), D0 + D_STEPS * last + u)

        @block.vector
        def _(dve):
            start(dve, (yb_ready, merged, y_ready, mg_lo_ready, u_ready), FIRST)
            base, turn, per, k = [0], [None], [0], [0]

            def step(ins):
                ins.then_inc(chain, 1)
                k[0] += 1
                dve.wait_ge(chain, base[0] + k[0] if turn[0] is None else turn[0] * per[0] + base[0] + k[0])

            def enter(i, n):
                base[0], k[0] = base[0] + k[0], 0
                turn[0], per[0] = i, n

            def leave(turns):
                assert k[0] == per[0], (k[0], per[0])
                base[0], k[0], turn[0] = base[0] + turns * per[0], 0, None

            dve.memset(c_parts[:].bitcast(F32), 0.0).then_inc(zeroed, 1)
            dve.memset(early_hi[:].bitcast(F32), 0.0).then_inc(zeroed, 1)
            dve.memset(early_lo[:].bitcast(F32), 0.0).then_inc(zeroed, 1)
            dve.memset(other_hi[:].bitcast(F32), 0.0).then_inc(zeroed, 1)
            dve.memset(other_lo[:].bitcast(F32), 0.0).then_inc(zeroed, 1)
            dve.wait_ge(masks_ready, 1)
            dve.tensor_tensor(pick[:], ident[0:4, 0:2], ident[0:4, 2:4], ALU.add).then_inc(pick_ready, 1)
            dve.wait_ge(silu_c, 2)
            c_part = c_parts[:, 0:4 * KT].rearrange("p (k r) -> p k r", r=4)
            dve.tensor_tensor(c_part[:, :, 2:4], c_silu[:], c_part[:, :, 0:2].bitcast(F32), ALU.subtract).then_inc(parts_ready, 1)

            def lo(ready, slot):
                dve.wait_ge(hi_ready, ready)
                dve.tensor_tensor(w_lo[:, slot], w_raw[:, slot], w_hi[:, slot].bitcast(F32), ALU.subtract).then_inc(lo_ready, 1)

            for kt in range(1, KT):
                dve.wait_ge(sqx_ready, kt + 1)
                if kt > 1:
                    dve.wait_ge(sqx_used, kt)
                first = sq_x[:, 0] if kt == 1 else sum_x[:]
                dve.tensor_tensor(sum_x[:], first, sq_x[:, kt % 4], ALU.add).then_inc(sqx_used, 2 if kt == 1 else 1)
            for n in range(LEAD):
                lo(n + 1, n)

            dve.wait_ge(gp_done, 1)
            for bank, at in ((6, G_PAST), (7, G_PAST + 512)):
                dve.tensor_copy(g_rows[:, at:at + 512], ps[0:H, bank, :]).then_inc(g_rows_ready, 1)

            def mod_sums(k):
                m = 2 * k
                dve.wait_ge(cols_done, k + 1)
                dve.tensor_scalar(mod[:, m], ps[:, 1, 0:2], b_ada[:, bass.ds(m, 1)], None, ALU.add).then_inc(mod_ready, 1)
                dve.tensor_scalar(mod[:, m + 1], ps[:, 1, 2:4], b_ada[:, bass.ds(m + 1, 1)], 1.0, ALU.add, ALU.add).then_inc(mod_ready, 1)

            def mod_scale(k):
                dve.wait_ge(mod_ready, 3 * k + 2)
                dve.tensor_scalar(mod[:, 2 * k + 1], mod[:, 2 * k + 1], norm_g[:, bass.ds(k, 1)], None, ALU.mult).then_inc(mod_ready, 1)

            def modulate(k):
                m = 2 * k
                dve.wait_ge(mod_ready, 3 * k + 3)
                dve.wait_ge(xn_ready, k + 1)
                for lo_, hi_, s in ((0, NP, 0), (NP, T, 1)):
                    dve.tensor_scalar(x_t[:, k, lo_:hi_], x_t[:, k, lo_:hi_], mod[:, m + 1, s:s + 1],
                                      mod[:, m, s:s + 1], ALU.mult, ALU.add).then_inc(h_ready, 1)

            def ada_los(g, work):
                for u in range(4):
                    lo(4 * g + u + LEAD + 1, (u + LEAD) % RING)
                    work(u)

            def inverse_root(u):
                if u % 2:
                    if u == 1:
                        dve.wait_ge(rstdx_ready, 1)
                    half = rstd_x[:, u // 2 * HC:(u // 2 + 1) * HC]
                    dve.reciprocal(half, half).then_inc(rinv_ready, 1)

            def first_mod(u):
                if u == 2:
                    mod_sums(0)
                if u == 3:
                    mod_scale(0)

            ada_los(0, inverse_root)
            ada_los(1, first_mod)
            with dve.Fori(2, KT) as g:
                def mod_and_h(u):
                    if u == 0:
                        modulate(g - 2)
                    if u == 2:
                        mod_sums(g - 1)
                    if u == 3:
                        mod_scale(g - 1)
                ada_los(g, mod_and_h)
            modulate(KT - 2)
            mod_sums(KT - 1)
            mod_scale(KT - 1)
            modulate(KT - 1)

            def pre_lo(u):
                lo(PRE0 + u + LEAD + 1, (u + LEAD) % RING)

            pre_lo(0)
            dve.wait_ge(f_turned, 1)
            dve.tensor_tensor(z_f[:], ps[:, 2, 0:5 * H].rearrange("p (t h) -> p t h", h=H), b_f[:], ALU.add).then_inc(tile_evac, 1)
            dve.wait_ge(f_act, 3)
            dve.scalar_tensor_tensor(out=logf[:], in0=z_f[:], scalar=0.0, in1=e_f[:], op0=ALU.min, op1=ALU.subtract).then_inc(logf_ready, 1)
            pre_lo(1)
            dve.wait_ge(g_done, 1)
            for bank, at, n in ((2, 0, NP), (3, G_NEW, NS)):
                dve.tensor_scalar(g_rows[:, at:at + n], ps[0:H, bank, 0:n], -1.0, None, ALU.mult).then_inc(g_rows_ready, 1)
            pre_lo(2)
            pre_lo(3)
            dve.wait_ge(g_stored, 16)

            def conv_step(taps, out):
                for w in taps:
                    if w == 0:
                        step(dve.tensor_scalar(acc[:], ext[:, 0:ACCW], conv_w[:, 0:1], conv_w[:, W:W + 1], ALU.mult, ALU.add))
                    elif w < W - 1:
                        step(dve.scalar_tensor_tensor(out=acc[:], in0=ext[:, w:w + ACCW], scalar=conv_w[:, w:w + 1],
                                                      in1=acc[:], op0=ALU.mult, op1=ALU.add))
                    else:
                        for a0, n, c0 in ((0, NP, 0), (S_ST, NS, NP)):
                            dve.scalar_tensor_tensor(out=out[:, c0:c0 + n], in0=ext[:, w + a0:w + a0 + n],
                                                     scalar=conv_w[:, w:w + 1], in1=acc[:, a0:a0 + n],
                                                     op0=ALU.mult, op1=ALU.add).then_inc(conv_done, 1)

            CONV = [range(0, 4)] + [range(4 + 3 * j, 7 + 3 * j) for j in range(9)]
            CONV_STEPS = W - 1
            dve.memset(ext[:], 0.0).then_inc(zeroed, 1)
            dve.memset(conv_w[:], 0.0).then_inc(zeroed, 1)
            dve.memset(s_s[NS:P, 0:P], 0.0).then_inc(zeroed, 1)
            dve.wait_ge(zeroed, 8)

            with dve.Fori(0, H) as i:
                enter(i, CONV_STEPS + 2 + 2 * 5)

                def normed(n, dst):
                    dve.wait_ge(std_ready, 2 * i + n + 1)
                    step(dve.reciprocal(rs[:], rs[:]))
                    dve.scalar_tensor_tensor(out=dst[:], in0=dst[:], scalar=qk_g[:, n:n + 1], in1=rs[:],
                                             op0=ALU.mult, op1=ALU.mult).then_inc(qkn_ready, 1)

                def scores_in(n, dst, bank, bias):
                    dve.wait_ge(sc_done, 7 * i + n + 1)
                    m, w = dst.shape[0], dst.shape[1]
                    dve.scalar_tensor_tensor(out=dst, in0=ps[0:m, bank, 0:w], scalar=SCALE, in1=g_b[0:m, bias:bias + w],
                                             op0=ALU.mult, op1=ALU.add).then_inc(sc_evac, 1)

                def prepare(j, n, s, last, m):
                    dve.wait_ge(sc_evac, FIRST + 7 * i + n + 1)
                    step(dve.tensor_tensor(s[:, last:last + m], s[:, last:last + m], causal[0:m, 0:m], ALU.add))
                    step(dve.tensor_reduce(stat_max[0:m, j:j + 1], s[:, 0:last + m], AX.X, ALU.max))
                    dve.tensor_scalar(stat_neg[0:m, j:j + 1], stat_max[0:m, j:j + 1], -1.0, None, ALU.mult).then_inc(prep_done, 1)

                def normalise(j, s, m):
                    dve.wait_ge(exp_done, 5 * i + j + 1)
                    dve.reciprocal(stat_inv[0:m, j:j + 1], stat_sum[0:m, j:j + 1]).then_inc(inv_done, 1)
                    dve.wait_ge(inv_done, 5 * i + j + 1)
                    dve.tensor_scalar(s, s, stat_inv[0:m, j:j + 1], None, ALU.mult).then_inc(p_ready, 1)

                def attended(j):
                    dve.wait_ge(pv_done, FIRST + 5 * i + j + 1)
                    n = P if j < QB else NS
                    y = y_a[:, i, P * j:P * j + n]
                    dve.tensor_tensor(y, y, ps[:, V, 0:n], ALU.mult).then_inc(pv_evac, 1)

                for u in range(A_STEPS):
                    lo(A0 + A_STEPS * i + u + LEAD + 1, (u + LEAD) % RING)
                    if u == 0:
                        dve.wait_ge(u_ready, FIRST + 2 * i)
                        dve.wait_ge(cw_landed, FIRST_DMA + 32 * i)
                    if u == 3:
                        normed(0, qn)
                    if u == 5:
                        normed(1, kn)
                    if u == 7:
                        dve.wait_ge(g_landed, 16 * (i + 1))
                    if 8 <= u < 12:
                        normalise(u - 8, s_p[:, u % 2, 0:P * (u - 7)], P)
                    if 7 <= u < 11:
                        b = u - 7
                        scores_in(b, s_p[:, b % 2, 0:P * (b + 1)], X + b % 2, 0)
                        prepare(b, b, s_p[:, b % 2], P * b, P)
                    if u == 10:
                        dve.wait_ge(tile_evac, FIRST + 8 * i + 5)
                    if 10 <= u < 14:
                        attended(u - 10)
                    if u == 11:
                        scores_in(4, s_s[0:NS, 0:512], X, G_PAST)
                    if u == 12:
                        scores_in(5, s_s[0:NS, 512:1024], Y, G_PAST + 512)
                        dve.wait_ge(tile_evac, FIRST + 8 * i + 7)
                        dve.tensor_tensor(ext[:, PADW:S_ST], ext[:, PADW:S_ST], sig[:, 0:NP], ALU.mult).then_inc(u_ready, 1)
                        dve.tensor_tensor(ext[:, S_U:EXT], ext[:, S_U:EXT], sig[:, NP:T], ALU.mult).then_inc(u_ready, 1)
                    if u == 13:
                        scores_in(6, s_s[0:NS, PAST:PAST + NS], X, G_NEW)
                        prepare(4, 6, s_s[0:NS], PAST, NS)
                    if u == 14:
                        normalise(4, s_s[0:NS], NS)
                    if u < 10:
                        conv_step(CONV[u], cv[:, i])
                attended(4)
                leave(H)

            def b_los(t, work=lambda r: None):
                for r in range(2):
                    for u in (2 * r, 2 * r + 1):
                        lo(B0 + 4 * t + u + LEAD + 1, (u + LEAD) % RING)
                    work(r)

            dve.wait_ge(u_ready, FIRST + 2 * H)
            dve.wait_ge(cw_landed, FIRST_DMA + 32 * H)
            conv_of = [range(0, 8), range(8, 16), range(16, 24), range(24, 31)]
            for t in range(CENTRE_TURN):
                b_los(t, lambda r: conv_step(conv_of[2 * t + r], cv[:, H]))
            dve.wait_ge(mean_done, 1)
            dve.wait_ge(k_stored, FIRST_DMA + 16 * H)
            dve.wait_ge(v_stored, FIRST_DMA + 16 * H)
            dve.wait_ge(gb_stored, FIRST_DMA + 16 * H)
            dve.wait_ge(c_stored, FIRST_DMA + 32 * H)
            dve.tensor_scalar(halves(mu[:]), banks(X), 1.0 / (H * P), None, ALU.mult).then_inc(centred, 1)
            dve.wait_ge(centred, 1)
            with dve.Fori(CENTRE_TURN, LN_TURN) as t:
                def centre(r):
                    c = 2 * (t - CENTRE_TURN) + r
                    dve.tensor_tensor(cv[:, c + 1], cv[:, c + 1], mu[:], ALU.subtract).then_inc(centred, 1)
                    dve.wait_ge(ya_hi_ready, c + 1)
                    dve.tensor_tensor(ya_lo[:, c], y_a[:, c], ya_hi[:, c].bitcast(F32), ALU.subtract).then_inc(ya_lo_ready, 1)
                b_los(t, centre)
            dve.wait_ge(rstd_ready, 1)
            step(dve.reciprocal(rstd[:], rstd[:]))
            with dve.Fori(LN_TURN, B_TURNS) as t:
                def scale_c(r):
                    c = 2 * (t - LN_TURN) + r
                    dve.tensor_copy(ln_cur[:], ln_gb[:, c]).then_inc(lncur_ready, 1)
                    dve.wait_ge(lncur_ready, c + 1)
                    dve.tensor_tensor(cv[:, c + 1], cv[:, c + 1], rstd[:], ALU.mult).then_inc(scaled, 1)
                    dve.wait_ge(ln_silu, c + 1)
                    dve.wait_ge(gb_landed[r], 16 * (t - LN_TURN + 1))
                    dve.tensor_tensor(cv[:, c + 1], cv[:, c + 1], gb_in[:, r], ALU.mult).then_inc(yb_ready, 1)
                b_los(t, scale_c)
            with dve.Fori(0, H) as c:
                dve.wait_ge(yb_hi_ready, c + 1)
                dve.tensor_tensor(yb_lo[:, c], cv[:, c + 1], yb_hi[:, c].bitcast(F32), ALU.subtract).then_inc(yb_lo_ready, 1)

            with dve.Fori(0, KT // 2) as t:
                enter(t, 2)
                for u in range(4):
                    lo(C0 + 4 * t + u + LEAD + 1, (u + LEAD) % RING)
                for r in range(2):
                    j = 2 * t + r
                    bank = 4 * r
                    dve.wait_ge(w_used, C0 + 4 * t + r + 3)
                    dve.wait_ge(m_landed[r], 32 * (t + 1))
                    dve.wait_ge(mg_lo_ready, FIRST + j)
                    dve.tensor_tensor(halves(merge[:]), banks(bank), halves(m_in[:, r, 0]), ALU.mult).then_inc(c_evac, 1)
                    step(dve.tensor_tensor(halves(merge_b[:]), banks(bank + 2), halves(m_in[:, r, 1]), ALU.mult))
                    dve.wait_ge(c_evac, j + 1)
                    dve.tensor_tensor(merge[:], merge[:], merge_b[:], ALU.add).then_inc(merged, 1)
                    dve.wait_ge(mg_hi_ready, j + 1)
                    dve.tensor_tensor(mg_lo[:, j], merge[:], mg_hi[:, j].bitcast(F32), ALU.subtract).then_inc(mg_lo_ready, 1)
                leave(KT // 2)

            def out_tile(t, r):
                j = 2 * t + r
                dve.wait_ge(w_used, D0 + D_STEPS * t + 2 * r + 2)
                dve.wait_ge(xin_landed[r], 16 * (t + 1))
                dve.wait_ge(y_stored[r], FIRST_DMA + 16 * t)
                for bank, lo_, hi_, at, s in ((0, 0, HC, 0, 0), (1, 0, NP - HC, HC, 0), (1, NP - HC, HC, NP, 1)):
                    n = hi_ - lo_
                    dve.scalar_tensor_tensor(out=y_out[:, r, at:at + n], in0=ps[:, 2 * r + bank, lo_:hi_],
                                             scalar=gate[:, j, s:s + 1], in1=x_in[:, r, at:at + n],
                                             op0=ALU.mult, op1=ALU.add).then_inc(y_ready, 1)

            def gate_products(t, q):
                dve.wait_ge(gate_landed[q], 16 * (t + 1))
                if q == 0:
                    dve.wait_ge(gate_summed, FIRST + t)
                for kk in range(AK):
                    kt = AK * q + kk
                    w = gate_w[:, q, kk]
                    for n in range(2):
                        if kt == 0:
                            dve.tensor_scalar(gate_acc[:, n], w, c_silu[:, kt, n:n + 1], None, ALU.mult).then_inc(gate_step, 1)
                        else:
                            dve.wait_ge(gate_step, GATE_STEPS * t + 2 * kt + n - 1)
                            dve.scalar_tensor_tensor(out=gate_acc[:, n], in0=w, scalar=c_silu[:, kt, n:n + 1], in1=gate_acc[:, n],
                                                     op0=ALU.mult, op1=ALU.add).then_inc(gate_step, 1)

            def gate_cols(t):
                dve.wait_ge(gate_summed, FIRST + t + 1)
                for n in range(4):
                    dve.tensor_tensor(gate_diag[:, n], ps[:, X, P * n:P * (n + 1)], ident[:], ALU.mult).then_inc(gate_diag_ready, 1)
                dve.wait_ge(gate_diag_ready, 5 * t + 4)
                dve.tensor_reduce(gate_sum[:], gate_diag[:], AX.X, ALU.add).then_inc(gate_diag_ready, 1)
                dve.wait_ge(gate_diag_ready, 5 * t + 5)
                sums = gate_sum[:].rearrange("p (s m) -> p m s", m=2)
                for r in range(2):
                    j = 2 * t + r
                    dve.tensor_scalar(gate[:, j], sums[:, r], b_ada[:, bass.ds(j + 2 * KT, 1)], None,
                                      ALU.add).then_inc(gate_ready, 1)
                dve.wait_ge(gate_ready, 2 * t + 2)

            with dve.Fori(0, KT // 2 - 1) as t:
                for u in range(D_STEPS):
                    lo(D0 + D_STEPS * t + u + LEAD + 1, (u + LEAD) % RING)
                    if u < 2:
                        gate_products(t, 2 * u)
                        gate_products(t, 2 * u + 1)
                gate_cols(t)
                out_tile(t, 0)
                out_tile(t, 1)
            for u in range(D_STEPS - LEAD):
                lo(D0 + D_STEPS * (KT // 2 - 1) + u + LEAD + 1, (u + LEAD) % RING)
            for q in range(4):
                gate_products(KT // 2 - 1, q)
            gate_cols(KT // 2 - 1)
            for r in range(2):
                out_tile(KT // 2 - 1, r)

        @block.tensor
        def _(pe):
            start(pe, (pv_done, gate_summed), FIRST)
            pe.wait_ge(masks_ready, 4)
            pe.wait_ge(const_in, 16 * 7)
            for tt in range(CT):
                for t2 in range(tt, CT):
                    mm = pe.matmul(ps[0:H, 6 + tt // 4, P * (tt % 4):P * (tt % 4 + 1)], logf_past[:, t2], ones[:] if t2 > tt else after[:],
                                   start=(t2 == tt), stop=(t2 == CT - 1))
            mm.then_inc(gp_done, 1)
            pe.wait_ge(sqx_used, KT)
            for c in range(2):
                mm = pe.matmul(ps[:, X + c, 0:HC], ones[:], sum_x[:, c * HC:(c + 1) * HC], start=True, stop=True)
            mm.then_inc(sumx_done, 1)

            def columns(slot, ready, k0, bank, start, stop):
                pe.wait_ge(hi_ready, ready)
                pe.wait_ge(lo_ready, ready)
                for kk in range(AK):
                    cs = c_parts[:, 4 * (k0 + kk):4 * (k0 + kk) + P]
                    for n, w in enumerate((w_hi, w_lo)):
                        mm = pe.matmul(ps[:, bank, 0:AW], cs, w[:, slot, AW * kk:AW * (kk + 1)],
                                       start=(start and kk == 0 and n == 0), stop=(stop and kk == AK - 1 and n == 1))
                mm.then_inc(w_used, 1)

            def to_columns(group, bank, read):
                pe.wait_ge(rows_ready, group + 1)
                if read is not None:
                    pe.wait_ge(*read)
                for m in range(2):
                    mm = pe.matmul(ps[:, bank, 2 * m:2 * m + 2], ada_rows[:, P * m:P * (m + 1)], pick[:], start=True, stop=True)
                mm.then_inc(cols_done, 1)

            def three(out, w, kk, parts, start, stop):
                (whi, wlo), (xhi, xlo) = w, parts
                n = 0
                for wp, xp in ((whi, xhi), (whi, xlo), (wlo, xhi)):
                    for c in range(2):
                        mm = pe.matmul(out[:, c], wp[:, kk * P:(kk + 1) * P], xp[:, c * HC:(c + 1) * HC],
                                       start=(start and n == 0), stop=(stop and n == 2))
                    n += 1
                return mm

            def unit(ready, slot, bank, src, k0, start, stop, tiles_ready=None):
                pe.wait_ge(hi_ready, ready)
                pe.wait_ge(lo_ready, ready)
                for kk in range(UK):
                    if tiles_ready is not None:
                        pe.wait_ge(tiles_ready, kk + 1)
                    mm = three(banks(bank), (w_hi[:, slot], w_lo[:, slot]), kk, (src[0][:, k0 + kk], src[1][:, k0 + kk]),
                               start and kk == 0, stop and kk == UK - 1)
                mm.then_inc(w_used, 1)

            def early_products(k, first=False, last=False, e_hi=early_hi, e_lo=early_lo):
                pe.wait_ge(h_lo_ready, k + 1)
                pe.wait_ge(early_lo_ready, k + 1)
                for n, at in enumerate((EARLY * P, 0, P)):
                    for m, (wp, xp) in enumerate(((e_hi, h_hi), (e_hi, h_lo), (e_lo, h_hi))):
                        for c in range(2):
                            mm = pe.matmul(ps[:, 2 + 2 * n + c, 0:HC], wp[:, at:at + P], xp[:, k, c * HC:(c + 1) * HC],
                                           start=(first and m == 0), stop=(last and m == 2))
                    if last and n == 0:
                        mm.then_inc(f_done, 1)
                mm.then_inc(early_used, 1)

            pe.wait_ge(parts_ready, 1)
            pe.wait_ge(pick_ready, 1)

            def ada_group(g, turned=True, k=None, first=False, second_on=True):
                if turned:
                    pe.wait_ge(rows_ready, g)
                for u in range(4):
                    columns(u, 4 * g + u + 1, AK * u, 0, u == 0, u == 3)
                    if u == 1 and turned:
                        to_columns(g - 1, 1, (mod_ready, 3 * g - 4) if second_on else None)
                if k is not None:
                    early_products(k, first)

            ada_group(0, turned=False)
            ada_group(1, second_on=False)
            pe.wait_ge(g_rows_ready, 2)
            ada_group(2)
            ada_group(3, k=0, first=True)
            with pe.Fori(4, KT) as g:
                ada_group(g, k=g - 3)
            to_columns(KT - 1, 1, (mod_ready, 3 * KT - 4))
            early_products(KT - 3)
            pe.wait_ge(mod_ready, 3 * KT - 1)
            unit(PRE0 + 1, 0, 0, (h_hi, h_lo), 0, True, False)
            early_products(KT - 2, e_hi=other_hi, e_lo=other_lo)
            early_products(KT - 1, last=True)
            pe.wait_ge(f_rows_ready, 1)
            for tt in range(5):
                at = P * tt if tt < QB else T - P
                mm = pe.transpose(ps[:, 2, H * tt:H * (tt + 1)], f_rows[:, at:at + P], ident[0:H, 0:H])
            mm.then_inc(f_turned, 1)
            unit(PRE0 + 2, 1, 0, (h_hi, h_lo), UK, False, True)
            pe.wait_ge(logf_ready, 1)
            for tt in range(QB):
                for t2 in range(tt + 1):
                    pe.matmul(ps[0:H, 2, P * tt:P * (tt + 1)], logf[:, t2], ones[:] if t2 < tt else upto[:], start=(t2 == 0), stop=(t2 == tt))
            pe.matmul(ps[0:H, 3, 0:NS], logf[NS:P, QB], upto[NS:P, NS:P], start=True, stop=True).then_inc(g_done, 1)
            pe.wait_ge(pre_evac, 1)
            unit(PRE0 + 3, 2, 4, (h_hi, h_lo), 0, True, False)
            unit(PRE0 + 4, 3, 4, (h_hi, h_lo), UK, False, True)
            pe.wait_ge(g_rows_ready, 4)
            pe.wait_ge(pre_evac, 2)

            h_parts = (h_hi, h_lo)
            with pe.Fori(0, H) as i:
                def square_sum(n, bank):
                    pe.wait_ge(sq_ready, 2 * i + n + 1)
                    for c in range(2):
                        mm = pe.matmul(ps[:, bank + c, 0:HC], ones[:], sq[:, c * HC:(c + 1) * HC], start=True, stop=True)
                    mm.then_inc(ss_done, 1)

                def scores(n, bank, q, keys, evacuated):
                    pe.wait_ge(sc_evac, FIRST + 7 * i + evacuated)
                    pe.matmul(ps[0:q.shape[1], bank, 0:keys.shape[1]], q, keys, start=True, stop=True).then_inc(sc_done, 1)

                def prompt_scores(b):
                    scores(b, X + b % 2, qn[:, P * b:P * (b + 1)], kn[:, 0:P * (b + 1)], max(b - 1, 0))

                def turn_probs(b):
                    pe.wait_ge(p_ready, 5 * i + b + 1)
                    if b:
                        pe.wait_ge(pt_ready, 6 * i + b)
                    for j in range(b + 1):
                        mm = pe.transpose(ps[:, Z, P * j:P * (j + 1)], s_p[:, b % 2, P * j:P * (j + 1)], ident[:])
                    mm.then_inc(tr_done, 1)

                def values(b):
                    pe.wait_ge(pt_ready, 6 * i + b + 1)
                    pe.wait_ge(pv_evac, FIRST + 5 * i + b)
                    for j in range(b + 1):
                        mm = pe.matmul(ps[:, V, 0:P], v_tok[:, j], p_t[:, j], start=(j == 0), stop=(j == b))
                    mm.then_inc(pv_done, 1)

                for u in range(A_STEPS):
                    t, half = divmod(u, 2)
                    if half == 0:
                        pe.wait_ge(tile_evac, FIRST + 8 * i + t)
                    unit(A0 + A_STEPS * i + u + 1, u % RING, 2 * (t % 2), h_parts, UK * half, half == 0, half == 1)
                    if u == 2:
                        pe.wait_ge(pre_evac, M_PRE)
                        pe.wait_ge(pv_evac, FIRST + 5 * i)
                        square_sum(0, X)
                    if u == 4:
                        square_sum(1, Z)
                    if u == 6:
                        pe.wait_ge(tile_evac, FIRST + 8 * i + 4)
                        pe.wait_ge(std_ready, 2 * i + 2)
                        for j in range(QB):
                            pe.transpose(ps[:, Z, P * j:P * (j + 1)], vf[:, P * j:P * (j + 1)], ident[:])
                        pe.transpose(ps[0:NS, V, 0:P], vf[:, NP:T], ident[:]).then_inc(vt_done, 1)
                        pe.wait_ge(qkn_ready, FIRST + 2 * i + 2)
                        prompt_scores(0)
                    if u == 7:
                        prompt_scores(1)
                    if u == 8:
                        pe.wait_ge(vtok_ready, 2 * i + 2)
                        turn_probs(0)
                        prompt_scores(2)
                    if 9 <= u < 13:
                        values(u - 9)
                        if u < 12:
                            turn_probs(u - 8)
                    if u == 9:
                        prompt_scores(3)
                    if u == 10:
                        pe.wait_ge(past_landed, 32 * i + 16)
                        scores(4, X, qn[:, NP:T], past[:, 0:512], 3)
                    if u == 11:
                        scores(5, Y, qn[:, NP:T], past[:, 512:1024], 4)
                    if u == 12:
                        scores(6, X, qn[:, NP:T], kn[:, NP:T], 5)
                    if u == 14:
                        pe.wait_ge(p_ready, 5 * i + 5)
                        pe.wait_ge(pt_ready, 6 * i + 4)
                        pe.transpose(ps[:, Z, 0:P], s_s[:, 0:P], ident[:])
                        for j in range(1, CT):
                            pe.transpose(ps[:, Z, NS * j:NS * (j + 1)], s_s[0:NS, P * j:P * (j + 1)], ident[0:NS, 0:NS])
                        pe.transpose(ps[0:NS, X, 0:NS], s_s[0:NS, PAST:PAST + NS], ident[0:NS, 0:NS]).then_inc(tr_done, 1)
                    if u == 15:
                        pe.wait_ge(pt_ready, 6 * i + 6)
                        pe.wait_ge(pv_evac, FIRST + 5 * i + 4)
                        pe.wait_ge(past_landed, 32 * i + 32)
                        for j in range(CT):
                            pe.matmul(ps[:, V, 0:NS], past[:, P * j:P * (j + 1)], ps_t[:, j], start=(j == 0), stop=False)
                        pe.matmul(ps[:, V, 0:NS], v_tok[0:NS, QB], pn_t[:], start=False, stop=True).then_inc(pv_done, 1)

            def b_turn(t, work=lambda u: None):
                for u in range(4):
                    if u % 2 == 0:
                        pe.wait_ge(tile_evac, FIRST + 8 * H + 2 * t + u // 2)
                    unit(B0 + 4 * t + u + 1, u, 2 * (u // 2), h_parts, UK * (u % 2), u % 2 == 0, u % 2 == 1)
                    work(u)

            def column_sum(src, done):
                for c in range(2):
                    mm = pe.matmul(ps[:, X + c, 0:HC], ones[:], src[:, c * HC:(c + 1) * HC], start=True, stop=True)
                mm.then_inc(done, 1)

            with pe.Fori(0, CENTRE_TURN) as t:
                b_turn(t)
            def mean_sum(u):
                if u == 1:
                    pe.wait_ge(summed, FIRST + H + 1)
                    column_sum(ch_sum, mean_done)

            b_turn(CENTRE_TURN, mean_sum)
            with pe.Fori(CENTRE_TURN + 1, LN_TURN) as t:
                b_turn(t)
            pe.wait_ge(sq_summed, H + 1)
            column_sum(sq_sum, var_done)
            with pe.Fori(LN_TURN, B_TURNS) as t:
                b_turn(t)

            pe.wait_ge(tile_evac, FIRST + 8 * H + 2 * B_TURNS)
            pe.wait_ge(ya_lo_ready, H)
            pe.wait_ge(rstd_ready, 1)

            def merge_turn(t, first=False):
                for r in range(2):
                    if not first:
                        pe.wait_ge(merged, FIRST + 2 * t + r - 1)
                    unit(C0 + 4 * t + r + 1, r, 4 * r, (ya_hi, ya_lo), 0, True, True)
                if first:
                    pe.wait_ge(tile_evac, FIRST + 8 * H + 2 * B_TURNS + 1)
                for r in range(2):
                    unit(C0 + 4 * t + r + 3, 2 + r, 4 * r + 2, (yb_hi, yb_lo), 0, True, True,
                         yb_lo_ready if first and r == 0 else None)

            merge_turn(0, first=True)
            with pe.Fori(1, KT // 2) as t:
                merge_turn(t)

            def out_turn(t, first=False):
                def part(u, r, half):
                    if half == 0 and not first:
                        pe.wait_ge(y_ready, FIRST + 6 * t + 3 * r - 3)
                    unit(D0 + D_STEPS * t + u + 1, u % RING, 2 * r, (mg_hi, mg_lo), UK * half, half == 0, half == 1)

                part(0, 0, 0)
                if first:
                    pe.wait_ge(mg_lo_ready, FIRST + KT)
                part(1, 0, 1)
                part(2, 1, 0)
                pe.wait_ge(gate_step, GATE_STEPS * (t + 1))
                if not first:
                    pe.wait_ge(gate_ready, 2 * t)
                pe.matmul(ps[:, X, 0:2 * AW], ones[:], gate_acc[:].rearrange("p s c -> p (s c)"), start=True, stop=True).then_inc(gate_summed, 1)
                part(3, 1, 1)

            pe.wait_ge(merged, FIRST + KT - 1)
            pe.wait_ge(mg_lo_ready, FIRST + UK)
            out_turn(0, first=True)
            with pe.Fori(1, KT // 2) as t:
                out_turn(t)


def kernel(**inp):
    import numpy as np
    import concourse.bacc as bacc
    from concourse.bass_utils import run_bass_kernel_spmd

    def cols(v):
        return v.reshape(-1, P).T

    def units(w):
        kk, nn = w.shape
        return w.reshape(kk // (P * UK), UK, P, nn // P, P).transpose(3, 0, 2, 1, 4).reshape(-1, P, UW)

    x = np.concatenate([inp["x_prompt"][0], inp["x_sample"][0]], 0)
    xt = x.T.reshape(KT, P, T)
    c = np.concatenate([inp["c_prompt"], inp["c_sample"]], 0)
    n_mod = 2 * KT
    order = [t for k in range(KT) for t in (k, KT + k)]
    ada = inp["w_ada"][0].reshape(KT // AK, AK, P, 3 * KT, P)[:, :, :, order + list(range(n_mod, 3 * KT))]
    ada = ada.reshape(KT // AK, AK, P, 3 * KT // 2, AW).transpose(3, 0, 2, 1, 4).reshape(3 * KT // 2, KT // AK, P, UW)
    b_cols = cols(inp["b_ada"][0])

    w_in = inp["w_in"][0]
    DA = H * P
    parts, at = {}, 0
    for name, n in (("q", DA), ("k", DA), ("v", DA), ("f", H), ("ga", DA), ("gl", DA), ("gg", DA), ("gb", DA), ("ma", D), ("mb", D)):
        parts[name] = w_in[:, at:at + n]
        at += n
    u = {n: units(p).reshape(-1, 2, P, UW) for n, p in parts.items() if n != "f"}
    turns = np.stack([u[n][:H] for n in ("q", "k", "v", "ga", "gl", "gg", "gb", "ma")], 1).reshape(-1, P, UW)
    rest = np.concatenate([u["ma"][H:], u["mb"]], 0)
    pre, rest = rest[EARLY:M_PRE].reshape(-1, P, UW), rest[M_PRE:].reshape(-1, P, UW)
    early = np.concatenate([parts["ma"][:, H * P:(H + EARLY) * P], parts["f"]], 1)
    w_o = np.concatenate([units(inp[n][0]).reshape(KT // 2, 2, P, UW) for n in ("w_oa", "w_ob")], 1).reshape(-1, P, UW)
    stream = np.concatenate([ada[:KT].reshape(-1, P, UW), pre, turns, rest, w_o, units(inp["w_out"][0])], 0)

    arrays = {
        "x": xt.transpose(1, 0, 2),
        "xt": xt,
        "c": c.T.reshape(KT, P, 2).transpose(1, 0, 2),
        "b_ada": np.concatenate([b_cols[:, order], b_cols[:, n_mod:]], 1),
        "norm_g": cols(inp["norm_g"][0]),
        "qk_g": np.stack([inp["q_norm_g"][0], inp["k_norm_g"][0]], 1),
        "ln_gb": np.stack([cols(inp["conv_ln_g"][0]), cols(inp["conv_ln_b"][0])], 2),
        "w_early": early.reshape(KT, P, EW).transpose(1, 0, 2),
        "b_f": np.broadcast_to(inp["b_f"][0], (P, 5, H)),
        "logf_past": inp["cache_logf"][0, 0].reshape(CT, P, H).transpose(1, 0, 2),
        "w": stream,
        "w_gate": ada[KT:].reshape(-1, P, AK, AW),
        "k_past": inp["cache_k"][0, 0].transpose(1, 2, 0),
        "v_past": inp["cache_v"][0, 0].reshape(CT, P, H, P).transpose(2, 1, 0, 3).reshape(H, P, PAST),
        "conv_w": np.concatenate([inp["conv_w"][0].T, inp["conv_b"][0][:, None]], 1).reshape(H, P, W + 1),
        "state": inp["state_conv"][0, 0].T.reshape(H, P, PADW),
    }
    outs = {"y": (KT, P, T), "k": (H, P, T), "v": (H, P, T), "logf_p": (P, QB, H), "logf_s": (NS, H),
            "conv_p": (H, P, PADW), "conv_s": (H, P, PADW)}
    nc = bacc.Bacc("TRN2", target_bir_lowering=False, num_devices=1, dynamic_dma_scratch_size=1024)
    feed, a, o = {}, {}, {}
    for name, v in arrays.items():
        feed[f"in_{name}"] = np.ascontiguousarray(v)
        a[name] = nc.dram_tensor(f"in_{name}", v.shape, F32, kind="ExternalInput").ap()
    for name, shape in outs.items():
        o[name] = nc.dram_tensor(f"out_{name}", shape, F32, kind="ExternalOutput").ap()
    build(nc, a, o)
    r = run_bass_kernel_spmd(nc, [feed], core_ids=[0]).results[0]
    got = {n: np.asarray(r[f"out_{n}"]) for n in outs}

    y = got["y"].reshape(D, T).T
    kv = {n: got[n].transpose(2, 0, 1) for n in ("k", "v")}
    conv = {n: got[n].reshape(DA, PADW).T[None, None] for n in ("conv_p", "conv_s")}
    return tuple(np.ascontiguousarray(v) for v in (
        y[None, :NP], y[None, NP:],
        kv["k"][None, None, :NP], kv["v"][None, None, :NP],
        got["logf_p"].transpose(1, 0, 2).reshape(1, 1, NP, H), conv["conv_p"],
        kv["k"][None, None, NP:], kv["v"][None, None, NP:],
        got["logf_s"][None, None], conv["conv_s"]))
```
